# Optimizing a Trainium2 kernel written in Bass

```python
import math
import jax, jax.numpy as jnp
from jax import lax
import numpy as np
import jax
import jax.numpy as jnp

D_MODEL = 1024
BATCH = 1
SEQ = 256
DEPTH = 2

GRID_W = 64
CTX_LEN = 256
N_EVEN = (DEPTH + 1) // 2
N_ODD = DEPTH // 2
EPS = 1e-6
ADA_CHUNKS = 6

H_A = 8
Q_LORA = 256
KV_LORA = 128
NOPE_DIM = 64
ROPE_DIM = 32
QK_DIM = NOPE_DIM + ROPE_DIM
V_DIM = 64
ROPE_BASE = 10000.0
Q_BLOCK = 128

H_R = 8
DK_R = 64
DV_R = 64
RET_CHUNK = 128
RET_W = H_R * DK_R

MLA_IN = Q_LORA + KV_LORA + ROPE_DIM
IN_WIDTH = MLA_IN + 4 * RET_W
MIX_W = H_A * V_DIM + H_R * DV_R

S5_GROUP = 16
S5_GROUPS = D_MODEL // S5_GROUP
S5_STATE = 64
S5_CHUNK = 128
DT_MIN = 1e-3
DT_MAX = 1e-1

D_FF = 4 * D_MODEL


def rmsnorm(x, g):
    xf = x.astype(jnp.float32)
    y = xf * lax.rsqrt(jnp.mean(xf * xf, axis=-1, keepdims=True) + EPS)
    return (y * g.astype(jnp.float32)).astype(x.dtype)

def head_norm(o):
    mu = jnp.mean(o, axis=-1, keepdims=True)
    var = jnp.mean(jnp.square(o - mu), axis=-1, keepdims=True)
    return (o - mu) * lax.rsqrt(var + EPS)

def modulate(h, shift, scale):
    return h * (1 + scale) + shift

def apply_rotary(x, ang):
    half = x.shape[-1] // 2
    cos = jnp.cos(ang)[None, :, None, :].astype(x.dtype)
    sin = jnp.sin(ang)[None, :, None, :].astype(x.dtype)
    x1, x2 = x[..., :half], x[..., half:]
    return jnp.concatenate([x1 * cos - x2 * sin, x1 * sin + x2 * cos], axis=-1)

def axial_angles(n_tok):
    rows = n_tok // GRID_W
    r = jnp.repeat(jnp.arange(rows, dtype=jnp.float32), GRID_W)
    col = jnp.tile(jnp.arange(GRID_W, dtype=jnp.float32), rows)
    nf = ROPE_DIM // 4
    f = ROPE_BASE ** (-jnp.arange(nf, dtype=jnp.float32) / nf)
    return jnp.concatenate([r[:, None] * f, col[:, None] * f], axis=-1)

def retnet_angles(n_tok):
    nf = DK_R // 2
    theta = ROPE_BASE ** (-jnp.arange(nf, dtype=jnp.float32) / nf)
    return jnp.arange(n_tok, dtype=jnp.float32)[:, None] * theta

def squared_relu_mlp(h, w1, w2):
    return jnp.square(jax.nn.relu(h @ w1)) @ w2

def mla_heads(z, q_norm_g, w_uq, kv_norm_g, w_ukv, qn_g, kn_g, ang):
    b, t = z.shape[:2]
    cq = z[..., :Q_LORA]
    ckv = z[..., Q_LORA:Q_LORA + KV_LORA]
    kr = z[..., Q_LORA + KV_LORA:]
    q = (rmsnorm(cq, q_norm_g) @ w_uq).reshape(b, t, H_A, QK_DIM)
    kv = (rmsnorm(ckv, kv_norm_g) @ w_ukv).reshape(b, t, H_A, NOPE_DIM + V_DIM)
    k = jnp.concatenate([kv[..., :NOPE_DIM], jnp.broadcast_to(kr[:, :, None, :], (b, t, H_A, ROPE_DIM))], axis=-1)
    v = kv[..., NOPE_DIM:]
    q = rmsnorm(q, qn_g)
    k = rmsnorm(k, kn_g)
    if ang is not None:
        q = jnp.concatenate([q[..., :NOPE_DIM], apply_rotary(q[..., NOPE_DIM:], ang)], axis=-1)
        k = jnp.concatenate([k[..., :NOPE_DIM], apply_rotary(k[..., NOPE_DIM:], ang)], axis=-1)
    return q, k, v

def attend(q, k, v):
    s = jnp.einsum('bqhd,bkhd->bhqk', q, k).astype(jnp.float32) * (QK_DIM ** -0.5)
    p = jax.nn.softmax(s, axis=-1).astype(v.dtype)
    return jnp.einsum('bhqk,bkhd->bqhd', p, v)

def blocked_attend(q, k, v):
    b, n_tok = q.shape[:2]
    nb = n_tok // Q_BLOCK
    qb = q.reshape(b, nb, Q_BLOCK, H_A, QK_DIM).swapaxes(0, 1)
    o = lax.map(lambda qq: attend(qq, k, v), qb)
    return o.swapaxes(0, 1).reshape(b, n_tok, H_A * V_DIM)

def ret_heads(z, ang):
    b, t = z.shape[:2]
    rq, rk, rv, rg = jnp.split(z, 4, axis=-1)
    rq = rq.reshape(b, t, H_R, DK_R).astype(jnp.float32)
    rk = rk.reshape(b, t, H_R, DK_R).astype(jnp.float32)
    rv = rv.reshape(b, t, H_R, DV_R).astype(jnp.float32)
    if ang is not None:
        rq = apply_rotary(rq, ang)
        rk = apply_rotary(rk, ang)
    return rq, rk * (DK_R ** -0.5), rv, rg

def retention_scan(q, k, v, log_gamma, s0, strict):
    b, t, h, _ = q.shape
    dv = v.shape[-1]
    n = t // RET_CHUNK
    i = jnp.arange(RET_CHUNK, dtype=jnp.float32)
    diff = i[:, None] - i[None, :]
    mask = (diff > 0) if strict else (diff >= 0)
    intra_decay = jnp.where(mask[None], jnp.exp(jnp.where(mask, diff, 0.0)[None] * log_gamma[:, None, None]), 0.0)
    q_decay = jnp.exp((i + 1)[:, None] * log_gamma[None])
    k_decay = jnp.exp((RET_CHUNK - 1 - i)[:, None] * log_gamma[None])
    chunk_decay = jnp.exp(RET_CHUNK * log_gamma)

    def blocks(a):
        return a.reshape(b, n, RET_CHUNK, h, a.shape[-1]).swapaxes(0, 1)

    def step(s, qkv):
        qc, kc, vc = qkv
        scores = jnp.einsum('bihd,bjhd->bhij', qc, kc) * intra_decay
        o = jnp.einsum('bhij,bjhe->bihe', scores, vc) + jnp.einsum('bihd,bhde->bihe', qc, s) * q_decay[None, :, :, None]
        s = s * chunk_decay[None, :, None, None] + jnp.einsum('bjhd,bjhe->bhde', kc * k_decay[None, :, :, None], vc)
        return s, o

    s_final, o = lax.scan(step, s0, (blocks(q), blocks(k), blocks(v)))
    return o.swapaxes(0, 1).reshape(b, t, h, dv), s_final

def ret_out(o, g):
    b, t = o.shape[:2]
    return head_norm(o).reshape(b, t, H_R * DV_R).astype(g.dtype) * jax.nn.silu(g)

def mla_retention_mixer(h_c, h_l, w_in, q_norm_g, w_uq, kv_norm_g, w_ukv, qn_g, kn_g, lg_f_raw, lg_b_raw, w_out, need_ctx):
    b, n_lat = h_l.shape[:2]
    z_c = h_c @ w_in
    z_l = h_l @ w_in
    q_c, k_c, v_c = mla_heads(z_c[..., :MLA_IN], q_norm_g, w_uq, kv_norm_g, w_ukv, qn_g, kn_g, None)
    q_l, k_l, v_l = mla_heads(z_l[..., :MLA_IN], q_norm_g, w_uq, kv_norm_g, w_ukv, qn_g, kn_g, axial_angles(n_lat))
    k_all = jnp.concatenate([k_c, k_l], axis=1)
    v_all = jnp.concatenate([v_c, v_l], axis=1)
    a_l = blocked_attend(q_l, k_all, v_all)
    lg_f = jnp.log1p(-jnp.exp2(lg_f_raw.astype(jnp.float32)))
    lg_b = jnp.log1p(-jnp.exp2(lg_b_raw.astype(jnp.float32)))
    rq_c, rk_c, rv_c, rg_c = ret_heads(z_c[..., MLA_IN:], None)
    rq_l, rk_l, rv_l, rg_l = ret_heads(z_l[..., MLA_IN:], retnet_angles(n_lat))
    zero = jnp.zeros((b, H_R, DK_R, DV_R), jnp.float32)
    o_cf, s_cf = retention_scan(rq_c, rk_c, rv_c, lg_f, zero, False)
    o_cb, s_cb = retention_scan(rq_c[:, ::-1], rk_c[:, ::-1], rv_c[:, ::-1], lg_b, zero, True)
    o_lf, _ = retention_scan(rq_l, rk_l, rv_l, lg_f, s_cf, False)
    o_lb, _ = retention_scan(rq_l[:, ::-1], rk_l[:, ::-1], rv_l[:, ::-1], lg_b, s_cb, True)
    r_l = ret_out(o_lf + o_lb[:, ::-1], rg_l)
    y_l = jnp.concatenate([a_l, r_l.astype(a_l.dtype)], axis=-1) @ w_out
    if need_ctx:
        a_c = attend(q_c, k_c, v_c).reshape(b, h_c.shape[1], H_A * V_DIM)
        r_c = ret_out(o_cf + o_cb[:, ::-1], rg_c)
        y_c = jnp.concatenate([a_c, r_c.astype(a_c.dtype)], axis=-1) @ w_out
    else:
        y_c = None
    return y_c, y_l

def s5_discretize(a_re, a_im, b_re, b_im, c_re, c_im, log_dt):
    f = lambda t: t.astype(jnp.float32)
    a = lax.complex(f(a_re), f(a_im))
    dt = jnp.exp(f(log_dt))[:, None]
    a_bar = jnp.exp(dt * a)
    b_bar = ((a_bar - 1) / a)[..., None] * lax.complex(f(b_re), f(b_im))
    c_mat = lax.complex(f(c_re), f(c_im))
    return a_bar, b_bar, c_mat

def _affine_compose(e1, e2):
    a1, b1 = e1
    a2, b2 = e2
    return a1 * a2, a2 * b1 + b2

def s5_scan(u, a_bar, b_bar, c_mat, x0):
    b, t = u.shape[:2]
    n = t // S5_CHUNK
    ub = u.reshape(b, n, S5_CHUNK, S5_GROUPS, S5_GROUP).swapaxes(0, 1)

    def step(x, u_blk):
        bu = jnp.einsum('btgh,gph->btgp', u_blk.astype(jnp.complex64), b_bar)
        bu = bu.at[:, 0].add(a_bar * x)
        a = jnp.broadcast_to(a_bar, bu.shape)
        _, xs = lax.associative_scan(_affine_compose, (a, bu), axis=1)
        y = jnp.einsum('btgp,ghp->btgh', xs, c_mat).real
        return xs[:, -1], y

    x_final, ys = lax.scan(step, x0, ub)
    return ys.swapaxes(0, 1).reshape(b, t, S5_GROUPS, S5_GROUP), x_final

def s5_out(y, u, d_skip, w_glu, dtype):
    b, t = u.shape[:2]
    y = (y + d_skip.astype(jnp.float32).reshape(S5_GROUPS, S5_GROUP) * u).reshape(b, t, D_MODEL)
    z = jax.nn.gelu(y).astype(dtype) @ w_glu
    za, zb = jnp.split(z, 2, axis=-1)
    return za * jax.nn.sigmoid(zb)

def s5_mixer(h_c, h_l, p_f, p_b, d_skip, w_glu, need_ctx):
    ab_f, bb_f, c_f = s5_discretize(*p_f)
    ab_b, bb_b, c_b = s5_discretize(*p_b)
    b = h_l.shape[0]
    u_c = h_c.astype(jnp.float32).reshape(b, h_c.shape[1], S5_GROUPS, S5_GROUP)
    u_l = h_l.astype(jnp.float32).reshape(b, h_l.shape[1], S5_GROUPS, S5_GROUP)
    x0 = jnp.zeros((b, S5_GROUPS, S5_STATE), jnp.complex64)
    y_cf, x_cf = s5_scan(u_c, ab_f, bb_f, c_f, x0)
    y_cb, x_cb = s5_scan(u_c[:, ::-1], ab_b, bb_b, c_b, x0)
    y_lf, _ = s5_scan(u_l, ab_f, bb_f, c_f, x_cf)
    y_lb, _ = s5_scan(u_l[:, ::-1], ab_b, bb_b, c_b, x_cb)
    out_l = s5_out(y_lf + y_lb[:, ::-1], u_l, d_skip, w_glu, h_l.dtype)
    out_c = s5_out(y_cf + y_cb[:, ::-1], u_c, d_skip, w_glu, h_c.dtype) if need_ctx else None
    return out_c, out_l

def first_inputs(seed: int = 0) -> dict:
    key = jax.random.key(seed)
    ks = iter(jax.random.split(key, 48))
    f32 = jnp.float32

    def nrm(shape, scale=1.0):
        return jax.random.normal(next(ks), shape, f32) * scale

    def gain(shape):
        return 1.0 + nrm(shape, 0.02)

    D = D_MODEL
    G, P, Hg = S5_GROUPS, S5_STATE, S5_GROUP
    n_idx = jnp.arange(P, dtype=f32)
    decay_init = -(5.0 + jnp.arange(H_R, dtype=f32))
    inputs = {
        'x': nrm((BATCH, SEQ, D)),
        'c': nrm((BATCH, D)),
        'ctx': nrm((BATCH, CTX_LEN, D)),
        'c_ctx': nrm((D,)),
        'ada_w': nrm((DEPTH, D, ADA_CHUNKS * D), 0.5 * D ** -0.5),
        'ada_b': nrm((DEPTH, ADA_CHUNKS * D), 0.02),
        'norm1_g': gain((DEPTH, D)),
        'norm2_g': gain((DEPTH, D)),
        'mlp_w1': nrm((DEPTH, D, D_FF), D ** -0.5),
        'mlp_w2': nrm((DEPTH, D_FF, D), D_FF ** -0.5),
        'w_in': nrm((N_EVEN, D, IN_WIDTH), D ** -0.5),
        'mla_q_norm_g': gain((N_EVEN, Q_LORA)),
        'mla_w_uq': nrm((N_EVEN, Q_LORA, H_A * QK_DIM), Q_LORA ** -0.5),
        'mla_kv_norm_g': gain((N_EVEN, KV_LORA)),
        'mla_w_ukv': nrm((N_EVEN, KV_LORA, H_A * (NOPE_DIM + V_DIM)), KV_LORA ** -0.5),
        'mla_qn_g': gain((N_EVEN, QK_DIM)),
        'mla_kn_g': gain((N_EVEN, QK_DIM)),
        'ret_lg_f': decay_init + nrm((N_EVEN, H_R), 0.1),
        'ret_lg_b': decay_init + nrm((N_EVEN, H_R), 0.1),
        'w_out': nrm((N_EVEN, MIX_W, D), MIX_W ** -0.5),
    }
    for d in ('f', 'b'):
        inputs['s5_a_re_' + d] = -0.5 + nrm((N_ODD, G, P), 0.01)
        inputs['s5_a_im_' + d] = jnp.pi * n_idx + nrm((N_ODD, G, P), 0.01)
        inputs['s5_b_re_' + d] = nrm((N_ODD, G, P, Hg), (2 * Hg) ** -0.5)
        inputs['s5_b_im_' + d] = nrm((N_ODD, G, P, Hg), (2 * Hg) ** -0.5)
        inputs['s5_c_re_' + d] = nrm((N_ODD, G, Hg, P), P ** -0.5)
        inputs['s5_c_im_' + d] = nrm((N_ODD, G, Hg, P), P ** -0.5)
        inputs['s5_log_dt_' + d] = math.log(DT_MIN) + jax.random.uniform(next(ks), (N_ODD, G), f32) * (math.log(DT_MAX) - math.log(DT_MIN))
    inputs['s5_d'] = nrm((N_ODD, D))
    inputs['s5_w_glu'] = nrm((N_ODD, D, 2 * D), D ** -0.5)
    return inputs

def first_block(x, c, ctx, c_ctx, ada_w, ada_b, norm1_g, norm2_g, mlp_w1, mlp_w2, w_in, mla_q_norm_g, mla_w_uq, mla_kv_norm_g, mla_w_ukv, mla_qn_g, mla_kn_g, ret_lg_f, ret_lg_b, w_out, s5_a_re_f, s5_a_im_f, s5_b_re_f, s5_b_im_f, s5_c_re_f, s5_c_im_f, s5_log_dt_f, s5_a_re_b, s5_a_im_b, s5_b_re_b, s5_b_im_b, s5_c_re_b, s5_c_im_b, s5_log_dt_b, s5_d, s5_w_glu):
    xc = ctx
    b = x.shape[0]
    for l in range(DEPTH):
        need_ctx = l < DEPTH - 1
        mod_l = (jax.nn.silu(c) @ ada_w[l] + ada_b[l]).reshape(b, ADA_CHUNKS, 1, D_MODEL)
        mod_c = (jax.nn.silu(c_ctx) @ ada_w[l] + ada_b[l]).reshape(ADA_CHUNKS, D_MODEL)
        h_l = modulate(rmsnorm(x, norm1_g[l]), mod_l[:, 0], mod_l[:, 1])
        h_c = modulate(rmsnorm(xc, norm1_g[l]), mod_c[0], mod_c[1])
        if l % 2 == 0:
            e = l // 2
            o_c, o_l = mla_retention_mixer(h_c, h_l, w_in[e], mla_q_norm_g[e], mla_w_uq[e], mla_kv_norm_g[e], mla_w_ukv[e], mla_qn_g[e], mla_kn_g[e], ret_lg_f[e], ret_lg_b[e], w_out[e], need_ctx)
        else:
            o = l // 2
            p_f = (s5_a_re_f[o], s5_a_im_f[o], s5_b_re_f[o], s5_b_im_f[o], s5_c_re_f[o], s5_c_im_f[o], s5_log_dt_f[o])
            p_b = (s5_a_re_b[o], s5_a_im_b[o], s5_b_re_b[o], s5_b_im_b[o], s5_c_re_b[o], s5_c_im_b[o], s5_log_dt_b[o])
            o_c, o_l = s5_mixer(h_c, h_l, p_f, p_b, s5_d[o], s5_w_glu[o], need_ctx)
        x = x + mod_l[:, 2] * o_l
        h_l = modulate(rmsnorm(x, norm2_g[l]), mod_l[:, 3], mod_l[:, 4])
        x = x + mod_l[:, 5] * squared_relu_mlp(h_l, mlp_w1[l], mlp_w2[l])
        if need_ctx:
            xc = xc + mod_c[2] * o_c
            h_c = modulate(rmsnorm(xc, norm2_g[l]), mod_c[3], mod_c[4])
            xc = xc + mod_c[5] * squared_relu_mlp(h_c, mlp_w1[l], mlp_w2[l])
    return x


D_MIX = D_MODEL
POOL_WIDTH = D_MIX // 4
POOL_WINDOWS = (2, 4, 8, 16)
POOL_GROUP_DIM = POOL_WIDTH // len(POOL_WINDOWS)
NSA_WIDTH = D_MIX - POOL_WIDTH
N_Q_HEADS = 8
HEAD_DIM = NSA_WIDTH // N_Q_HEADS
N_KV_GROUPS = 2
HEADS_PER_GROUP = N_Q_HEADS // N_KV_GROUPS
KV_WIDTH = N_KV_GROUPS * HEAD_DIM
N_BRANCHES = 3
CMP_STRIDE = 16
CMP_BLOCK = 2 * CMP_STRIDE
SLC_BLOCK = 64
N_SELECT = 16
WINDOW = 512
D_FF_2 = 2816
D_IN = POOL_WIDTH + NSA_WIDTH + 6 * KV_WIDTH + N_BRANCHES * N_Q_HEADS
ALPHA = (2.0 * DEPTH) ** 0.25
BETA = (8.0 * DEPTH) ** -0.25
LN_EPS = 1e-5
NEG_BIG = -1e30
SEL_BIG = 1e30


def layer_norm(x, g, b):
    xf = x.astype(jnp.float32)
    mu = jnp.mean(xf, axis=-1, keepdims=True)
    var = jnp.mean(jnp.square(xf - mu), axis=-1, keepdims=True)
    y = (xf - mu) * lax.rsqrt(var + LN_EPS) * g.astype(jnp.float32) + b.astype(jnp.float32)
    return y.astype(x.dtype)

def swiglu(x, w_gate, w_up, w_down):
    return (jax.nn.silu(x @ w_gate) * (x @ w_up)) @ w_down

def masked_softmax(s, mask):
    s = jnp.where(mask, s, NEG_BIG)
    m = jnp.max(s, axis=-1, keepdims=True)
    e = jnp.exp(s - m) * mask
    return e / jnp.maximum(jnp.sum(e, axis=-1, keepdims=True), 1e-30)

def pool_mixer(u, pool_w, pool_scale):
    B, S, _ = u.shape
    uf = u.astype(jnp.float32)
    csum = jnp.pad(jnp.cumsum(uf, axis=1), ((0, 0), (1, 0), (0, 0)))
    t = jnp.arange(S)
    groups = []
    for g, w in enumerate(POOL_WINDOWS):
        sl = slice(g * POOL_GROUP_DIM, (g + 1) * POOL_GROUP_DIM)
        cg = csum[..., sl]
        lo = jnp.maximum(t + 1 - w, 0)
        win_sum = cg[:, 1:] - cg[:, lo]
        cnt = jnp.minimum(t + 1, w).astype(jnp.float32)[None, :, None]
        groups.append(win_sum / cnt - uf[..., sl])
    pooled = jnp.stack(groups, axis=2).astype(u.dtype)
    mixed = jnp.einsum('bsgc,gcd->bsgd', pooled, pool_w)
    return mixed.reshape(B, S, POOL_WIDTH) * pool_scale

def compress(kv, pos, w1, w2):
    B, G, S, dh = kv.shape
    chunks = kv.reshape(B, G, S // CMP_STRIDE, CMP_STRIDE, dh)
    blocks = jnp.concatenate([chunks[:, :, :-1], chunks[:, :, 1:]], axis=3)
    flat = (blocks + pos).reshape(B, G, S // CMP_STRIDE - 1, CMP_BLOCK * dh)
    return jax.nn.gelu(flat @ w1) @ w2

def nsa_mixer(q, kc, vc, k_slc, v_slc, k_win, v_win, gates):
    B, S = q.shape[0], q.shape[1]
    G = N_KV_GROUPS
    NQB = S // Q_BLOCK
    NS = S // SLC_BLOCK
    NC = S // CMP_STRIDE - 1
    n_sel = min(N_SELECT, NS)
    scale = HEAD_DIM ** -0.5
    qb = (q * scale).reshape(B, NQB, Q_BLOCK, G, HEADS_PER_GROUP, HEAD_DIM).transpose(1, 0, 3, 4, 2, 5)
    gb = gates.reshape(B, NQB, Q_BLOCK, G, HEADS_PER_GROUP, N_BRANCHES).transpose(1, 0, 3, 4, 2, 5)
    ks_blocks = k_slc.reshape(B, G, NS, SLC_BLOCK, HEAD_DIM)
    vs_blocks = v_slc.reshape(B, G, NS, SLC_BLOCK, HEAD_DIM)
    kw_pad = jnp.pad(k_win, ((0, 0), (0, 0), (WINDOW, 0), (0, 0)))
    vw_pad = jnp.pad(v_win, ((0, 0), (0, 0), (WINDOW, 0), (0, 0)))
    cmp_end = jnp.arange(NC) * CMP_STRIDE + CMP_BLOCK - 1
    blk = jnp.arange(NS)
    bi = jnp.arange(B)[:, None, None, None]
    gi = jnp.arange(G)[None, :, None, None]
    slc_w = jnp.array([0.5, 1.0, 1.0, 1.0], jnp.float32)

    def one_block(args):
        c, q_c, g_c = args
        t = c * Q_BLOCK + jnp.arange(Q_BLOCK)
        s = jnp.einsum('bghtd,bgnd->bghtn', q_c, kc).astype(jnp.float32)
        p_cmp = masked_softmax(s, cmp_end[None, :] <= t[:, None])
        o_cmp = jnp.einsum('bghtn,bgnd->bghtd', p_cmp.astype(vc.dtype), vc)
        imp = jnp.pad(p_cmp.sum(axis=2), ((0, 0), (0, 0), (0, 0), (1, 1)))
        imp_slc = imp[..., :4 * NS].reshape(B, G, Q_BLOCK, NS, 4) @ slc_w + 0.5 * imp[..., 4::4]
        jt = (t // SLC_BLOCK)[:, None]
        forced = (blk == 0) | (blk == jt) | (blk == jt - 1)
        score = jnp.where(blk <= jt, jnp.where(forced, SEL_BIG, imp_slc), NEG_BIG)
        top_s, idx = lax.top_k(score, n_sel)
        sel_ok = top_s > 0.5 * NEG_BIG
        ks = ks_blocks[bi, gi, idx].reshape(B, G, Q_BLOCK, n_sel * SLC_BLOCK, HEAD_DIM)
        vs = vs_blocks[bi, gi, idx].reshape(B, G, Q_BLOCK, n_sel * SLC_BLOCK, HEAD_DIM)
        pos = (idx[..., None] * SLC_BLOCK + jnp.arange(SLC_BLOCK)).reshape(B, G, Q_BLOCK, n_sel * SLC_BLOCK)
        m_slc = (pos <= t[:, None]) & jnp.repeat(sel_ok, SLC_BLOCK, axis=-1)
        s = jnp.einsum('bghtd,bgtkd->bghtk', q_c, ks).astype(jnp.float32)
        p = masked_softmax(s, m_slc[:, :, None])
        o_slc = jnp.einsum('bghtk,bgtkd->bghtd', p.astype(vs.dtype), vs)
        start = c * Q_BLOCK
        kw = lax.dynamic_slice_in_dim(kw_pad, start, WINDOW + Q_BLOCK, axis=2)
        vw = lax.dynamic_slice_in_dim(vw_pad, start, WINDOW + Q_BLOCK, axis=2)
        s_pos = start - WINDOW + jnp.arange(WINDOW + Q_BLOCK)
        diff = t[:, None] - s_pos[None, :]
        m_win = (s_pos[None, :] >= 0) & (diff >= 0) & (diff < WINDOW)
        s = jnp.einsum('bghtd,bgkd->bghtk', q_c, kw).astype(jnp.float32)
        p = masked_softmax(s, m_win)
        o_win = jnp.einsum('bghtk,bgkd->bghtd', p.astype(vw.dtype), vw)
        o = g_c[..., 0:1] * o_cmp + g_c[..., 1:2] * o_slc + g_c[..., 2:3] * o_win
        return o.transpose(0, 3, 1, 2, 4).reshape(B, Q_BLOCK, NSA_WIDTH)

    out = lax.map(one_block, (jnp.arange(NQB), qb, gb))
    return out.transpose(1, 0, 2, 3).reshape(B, S, NSA_WIDTH)

def hybrid_mixer(x, w_in, b_gate, pool_w, pool_scale, cmp_pos_k, cmp_k_w1, cmp_k_w2,
                 cmp_pos_v, cmp_v_w1, cmp_v_w2, w_out):
    B, S, _ = x.shape
    proj = x @ w_in
    cuts = tuple(int(v) for v in np.cumsum([POOL_WIDTH, NSA_WIDTH] + [KV_WIDTH] * 6))
    u, q, kc, vc, ks, vs, kw, vw, g = jnp.split(proj, cuts, axis=-1)
    y_pool = pool_mixer(u, pool_w, pool_scale)

    def heads(a):
        return a.reshape(B, S, N_KV_GROUPS, HEAD_DIM).transpose(0, 2, 1, 3)

    k_cmp = compress(heads(kc), cmp_pos_k, cmp_k_w1, cmp_k_w2)
    v_cmp = compress(heads(vc), cmp_pos_v, cmp_v_w1, cmp_v_w2)
    gates = jax.nn.sigmoid((g + b_gate).astype(jnp.float32)).astype(x.dtype)
    gates = gates.reshape(B, S, N_Q_HEADS, N_BRANCHES)
    y_nsa = nsa_mixer(q.reshape(B, S, N_Q_HEADS, HEAD_DIM), k_cmp, v_cmp,
                      heads(ks), heads(vs), heads(kw), heads(vw), gates)
    return jnp.concatenate([y_pool, y_nsa], axis=-1) @ w_out

def second_inputs(seed: int = 0) -> dict:
    key = jax.random.key(seed)
    k = jax.random.split(key, 24)
    L = DEPTH

    def nrm(kk, shape, scale):
        return jax.random.normal(kk, shape, jnp.float32) * scale

    return {
        'x': nrm(k[0], (BATCH, SEQ, D_MODEL), 1.0),
        'ln1_g': 1.0 + nrm(k[1], (L, D_MODEL), 0.02),
        'ln1_b': nrm(k[2], (L, D_MODEL), 0.02),
        'ffn1_w_gate': nrm(k[3], (L, D_MODEL, D_FF_2), D_MODEL ** -0.5),
        'ffn1_w_up': nrm(k[4], (L, D_MODEL, D_FF_2), D_MODEL ** -0.5),
        'ffn1_w_down': nrm(k[5], (L, D_FF_2, D_MODEL), BETA * D_FF_2 ** -0.5),
        'w_in': nrm(k[6], (L, D_MODEL, D_IN), D_MODEL ** -0.5),
        'b_gate': nrm(k[7], (L, N_BRANCHES * N_Q_HEADS), 0.5),
        'pool_w': nrm(k[8], (L, len(POOL_WINDOWS), POOL_GROUP_DIM, POOL_GROUP_DIM), POOL_GROUP_DIM ** -0.5),
        'pool_scale': 1.0 + nrm(k[9], (L, POOL_WIDTH), 0.02),
        'cmp_pos_k': nrm(k[10], (L, CMP_BLOCK, HEAD_DIM), 0.02),
        'cmp_k_w1': nrm(k[11], (L, CMP_BLOCK * HEAD_DIM, HEAD_DIM), (CMP_BLOCK * HEAD_DIM) ** -0.5),
        'cmp_k_w2': nrm(k[12], (L, HEAD_DIM, HEAD_DIM), HEAD_DIM ** -0.5),
        'cmp_pos_v': nrm(k[13], (L, CMP_BLOCK, HEAD_DIM), 0.02),
        'cmp_v_w1': nrm(k[14], (L, CMP_BLOCK * HEAD_DIM, HEAD_DIM), (CMP_BLOCK * HEAD_DIM) ** -0.5),
        'cmp_v_w2': nrm(k[15], (L, HEAD_DIM, HEAD_DIM), HEAD_DIM ** -0.5),
        'w_out': nrm(k[16], (L, D_MIX, D_MODEL), BETA * D_MIX ** -0.5),
        'ln2_g': 1.0 + nrm(k[17], (L, D_MODEL), 0.02),
        'ln2_b': nrm(k[18], (L, D_MODEL), 0.02),
        'ffn2_w_gate': nrm(k[19], (L, D_MODEL, D_FF_2), D_MODEL ** -0.5),
        'ffn2_w_up': nrm(k[20], (L, D_MODEL, D_FF_2), D_MODEL ** -0.5),
        'ffn2_w_down': nrm(k[21], (L, D_FF_2, D_MODEL), BETA * D_FF_2 ** -0.5),
        'ln3_g': 1.0 + nrm(k[22], (L, D_MODEL), 0.02),
        'ln3_b': nrm(k[23], (L, D_MODEL), 0.02),
    }

def second_block(x, ln1_g, ln1_b, ffn1_w_gate, ffn1_w_up, ffn1_w_down, w_in, b_gate,
              pool_w, pool_scale, cmp_pos_k, cmp_k_w1, cmp_k_w2, cmp_pos_v, cmp_v_w1,
              cmp_v_w2, w_out, ln2_g, ln2_b, ffn2_w_gate, ffn2_w_up, ffn2_w_down,
              ln3_g, ln3_b):
    for l in range(DEPTH):
        x = layer_norm(ALPHA * x + 0.5 * swiglu(x, ffn1_w_gate[l], ffn1_w_up[l], ffn1_w_down[l]),
                       ln1_g[l], ln1_b[l])
        y = hybrid_mixer(x, w_in[l], b_gate[l], pool_w[l], pool_scale[l], cmp_pos_k[l],
                         cmp_k_w1[l], cmp_k_w2[l], cmp_pos_v[l], cmp_v_w1[l], cmp_v_w2[l], w_out[l])
        x = layer_norm(ALPHA * x + y, ln2_g[l], ln2_b[l])
        x = layer_norm(ALPHA * x + 0.5 * swiglu(x, ffn2_w_gate[l], ffn2_w_up[l], ffn2_w_down[l]),
                       ln3_g[l], ln3_b[l])
    return x


def setup_inputs(seed=0):
    out = dict(first_inputs(seed))
    for name, value in second_inputs(seed + 1).items():
        if name != "x":
            out[name + "_2"] = value
    return out


def reference(
    x, c, ctx, c_ctx, ada_w, ada_b, norm1_g, norm2_g, mlp_w1, mlp_w2, w_in, mla_q_norm_g,
    mla_w_uq, mla_kv_norm_g, mla_w_ukv, mla_qn_g, mla_kn_g, ret_lg_f, ret_lg_b, w_out,
    s5_a_re_f, s5_a_im_f, s5_b_re_f, s5_b_im_f, s5_c_re_f, s5_c_im_f, s5_log_dt_f, s5_a_re_b,
    s5_a_im_b, s5_b_re_b, s5_b_im_b, s5_c_re_b, s5_c_im_b, s5_log_dt_b, s5_d, s5_w_glu, ln1_g_2,
    ln1_b_2, ffn1_w_gate_2, ffn1_w_up_2, ffn1_w_down_2, w_in_2, b_gate_2, pool_w_2,
    pool_scale_2, cmp_pos_k_2, cmp_k_w1_2, cmp_k_w2_2, cmp_pos_v_2, cmp_v_w1_2, cmp_v_w2_2,
    w_out_2, ln2_g_2, ln2_b_2, ffn2_w_gate_2, ffn2_w_up_2, ffn2_w_down_2, ln3_g_2, ln3_b_2,
):
    x = first_block(
        x, c, ctx, c_ctx, ada_w, ada_b, norm1_g, norm2_g, mlp_w1, mlp_w2, w_in, mla_q_norm_g,
        mla_w_uq, mla_kv_norm_g, mla_w_ukv, mla_qn_g, mla_kn_g, ret_lg_f, ret_lg_b, w_out,
        s5_a_re_f, s5_a_im_f, s5_b_re_f, s5_b_im_f, s5_c_re_f, s5_c_im_f, s5_log_dt_f,
        s5_a_re_b, s5_a_im_b, s5_b_re_b, s5_b_im_b, s5_c_re_b, s5_c_im_b, s5_log_dt_b, s5_d,
        s5_w_glu,
    )
    return second_block(
        x, ln1_g_2, ln1_b_2, ffn1_w_gate_2, ffn1_w_up_2, ffn1_w_down_2, w_in_2, b_gate_2,
        pool_w_2, pool_scale_2, cmp_pos_k_2, cmp_k_w1_2, cmp_k_w2_2, cmp_pos_v_2, cmp_v_w1_2,
        cmp_v_w2_2, w_out_2, ln2_g_2, ln2_b_2, ffn2_w_gate_2, ffn2_w_up_2, ffn2_w_down_2,
        ln3_g_2, ln3_b_2,
    )


_drawn_inputs = setup_inputs


def setup_inputs(seed=0):
    import zlib

    import numpy as np

    out = dict(_drawn_inputs(seed))
    spreads = {}
    factors = {'norm1_g': 8.0,
     'norm2_g': 4.368,
     'mla_q_norm_g': 8.0,
     'mla_kv_norm_g': 8.0,
     'mla_qn_g': 8.0,
     'mla_kn_g': 8.0,
     's5_a_re_f': 64.0,
     's5_a_im_f': 40.112,
     's5_b_re_f': 53.896,
     's5_b_im_f': 58.088,
     's5_c_re_f': 54.288,
     's5_c_im_f': 56.384,
     's5_log_dt_f': 48.032,
     's5_a_re_b': 64.0,
     's5_a_im_b': 41.16,
     's5_b_re_b': 56.808,
     's5_b_im_b': 58.104,
     's5_c_re_b': 57.0,
     's5_c_im_b': 57.68,
     's5_log_dt_b': 48.416,
     'pool_scale_2': 22.99,
     'cmp_pos_k_2': 64.0,
     'cmp_pos_v_2': 41.588,
     'ln1_b_2': 3.453,
     'b_gate_2': 2.973,
     'cmp_k_w1_2': 3.662,
     'cmp_k_w2_2': 3.771}
    for name, (base, spread) in spreads.items():
        noise = np.random.default_rng([zlib.crc32(name.encode()), seed]).standard_normal(out[name].shape)
        drawn = base * np.exp(spread * noise) if base else spread * noise
        out[name] = jnp.asarray(drawn.astype(out[name].dtype))
    for name, factor in factors.items():
        out[name] = (out[name] * factor).astype(out[name].dtype)
    return out
```

```python
from contextlib import ExitStack, contextmanager

import numpy as np
import concourse.bass as bass
from concourse import mybir

F32 = mybir.dt.float32
ALU = mybir.AluOpType
ACT = mybir.ActivationFunctionType
AX = mybir.AxisListType
ds = bass.ds

P = 128
D = 1024
KT = D // P
N_LAT, N_CTX = 256, 256
TOK = N_LAT + N_CTX
TT, TL = TOK // P, N_LAT // P
DEPTH = 2
CHUNKS = 6
EPS, LN_EPS = 1e-6, 1e-5
H = 8
Q_LORA, KV_LORA, NOPE, ROPE, V_DIM = 256, 128, 64, 32, 64
QK = NOPE + ROPE
MLA_IN = Q_LORA + KV_LORA + ROPE
RD = 64
RET_W = H * RD
IN_W = MLA_IN + 4 * RET_W
D_FF = 4 * D
G, GH, GP = 64, 16, 64
CL = 8
NCH_L, NCH = N_LAT // CL, TOK // CL
LAGS = 2 * CL - 1
GB = P // GH
D_FF2 = 2816
FT2 = D_FF2 // P
POOL_W, POOL_G = 256, 64
WINDOWS = (2, 4, 8, 16)
HD = 96
KVW = 2 * HD
HPG = H // 2
D_IN2 = POOL_W + H * HD + 6 * KVW + 3 * H
CMP_S, CMP_L = 16, 32
NC = N_LAT // CMP_S - 1
ALPHA = (2.0 * DEPTH) ** 0.25
NEG = -1e30
SLOTS = 4
SLOT = 2048
TWO_PI = 2.0 * np.pi
BANKS = 8


def w_chunks(n_k):
    n = -(-n_k // 4)
    return [(a * n_k // n, (a + 1) * n_k // n) for a in range(n)]


class Lane:

    def __init__(self, name, engine, sem):
        self.name, self.engine, self.sem = name, engine, sem
        self.seen, self.index, self.per = {}, None, {}

    def due(self, name, k=1):
        self.seen[name] = self.seen.get(name, 0) + k
        if self.index is None:
            return self.seen[name]
        return self.seen[name] + self.index * self.per[name]

    @contextmanager
    def loop(self, count, **per):
        start = dict(self.seen)
        with self.engine.Fori(0, count) as i:
            self.index, self.per = i, per
            yield i
            self.index, self.per = None, {}
        for name, now in self.seen.items():
            was = start.get(name, 0)
            assert now - was == per.get(name, 0), (self.name, name, now - was, per.get(name, 0))
            self.seen[name] = was + count * (now - was)


class TensorLane(Lane):

    def __init__(self, name, engine, sem):
        super().__init__(name, engine, sem)
        self.held, self.given = {}, {"vector": BANKS, "scalar": BANKS}
        self.tile, self.first = 0, False

    def freed(self, bank):
        user, count = self.held.get(bank, ("vector", BANKS))
        return self.sem(user + "_released"), count

    def hand(self, banks, user):
        self.given[user] += 1
        for b in banks:
            self.held[b] = (user, self.given[user])

    @contextmanager
    def bank_loop(self, count, gives, **per):
        start, self.gives = self.given["vector"], gives
        self.start = start
        with self.loop(count, **per) as i:
            yield i
        assert self.given["vector"] - start == gives
        self.given["vector"] = start + count * gives
        self.held = {b: (r, n + (count - 1) * gives) for b, (r, n) in self.held.items()}

    def place_freed(self, place):
        return self.index * self.gives + (self.start - self.gives + place)




class Kernel:

    def __init__(self, nc, ctx, a):
        self.nc, self.a = nc, a
        self.sems = {}

        def sem(name):
            if name not in self.sems:
                self.sems[name] = ctx.enter_context(nc.semaphore(name))
            return self.sems[name]

        def sb(name, *shape):
            return ctx.enter_context(nc.sbuf_tensor(name, [P, *shape], F32))

        self.sem = sem
        self.x = sb("x_rows", TT, D)
        self.hT = sb("h_columns", KT, TOK)
        self.xn = sb("normed_rows", TT * D)
        self.big = sb("big", 16384)
        self.aux = sb("aux", 4096)
        self.ring = sb("weights", SLOTS, SLOT)
        self.rowv = sb("row_vectors", 2, D)
        self.modT = sb("modulation", DEPTH, CHUNKS * KT, 2)
        self.normT = sb("norm_scale", DEPTH, 2, 2, KT)
        self.ident = sb("identity", P)
        self.raw = sb("vectors_as_rows", 2, P)
        self.colp = sb("vectors_as_columns", 64)
        self.adab = sb("ada_bias", DEPTH * CHUNKS * KT)
        self.cs = sb("silu_c", KT, 2)
        self.sm = sb("statistics", 512)
        self.rope_mla = sb("rope_mla", TL, 2, ROPE // 2)
        self.rope_ret = sb("rope_ret", TL, 2, RD // 2)
        self.lag = sb("lag", 2, 3 * P)
        self.gains = sb("head_gains", 2, QK)
        self.lgr = sb("log_gamma", 6, 2 * H)
        self.dec = sb("decays", 4, H, 2)
        self.dlen = sb("decay_lengths", 4, 2)
        self.pw = sb("s5_powers", 2, CL + 1, G)
        self.s5p = sb("s5_parameters", 10, G)
        self.ps = ctx.enter_context(nc.psum_tensor("banks", [P, BANKS, 512], F32))
        self.scratch = nc.dram_tensor("s5_scratch_u", [D, CL, NCH], F32, kind="Internal").ap()
        self.scratch_y = nc.dram_tensor("s5_scratch_y", [P, G * NCH_L], F32, kind="Internal").ap()
        self.z = self.big[:, 0:TT * IN_W].rearrange("p (t n) -> p t n", t=TT)
        o = TT * IN_W
        self.kv = self.big[:, o:o + TT * H * P].rearrange("p (t h n) -> p t h n", t=TT, h=H)
        o += TT * H * P
        self.qkT = self.big[:, o:o + 2048].rearrange("p (b n t) -> p b n t", b=2, n=2)
        self.ro = self.big[:, o:o + 2048].rearrange("p (t h d) -> p t h d", t=TT, h=H)
        self.h1T = self.big[:, :].rearrange("p (f t) -> p f t", t=TOK)
        self.xnr = self.xn[:, :].rearrange("p (t n) -> p t n", t=TT)
        self.s5_ends = nc.dram_tensor("s5_ends", [G // GB, P, SLOT], F32, kind="Internal").ap()
        self.s5_out = nc.dram_tensor("s5_out", [G // GB, 2, P, 3 * 4 * P], F32, kind="Internal").ap()
        self.s5_places()
        self.s5_views()
        self.mixer2_views()
        self.slots = []


    def tile_begins(self, T):
        slot = T.tile % SLOTS
        T.tile += 1
        T.engine.wait_ge(self.sem(f"slot{slot}_loaded"), T.due(f"slot{slot}_loaded", 16))
        T.first = True
        return slot

    def mm(self, T, out, lhsT, rhs, start, stop):
        ins = T.engine.matmul(out, lhsT, rhs, start=start, stop=stop)
        if T.first:
            ins.then_inc(self.sem("weights_used"), 1)
            T.first = False
        return ins

    def load_rows_of(self, w, n_k, width, c0=0, rows=P, per=4):
        for k0, k1 in w_chunks(n_k) if per == 4 else [(0, n_k)]:
            src = w[k0 * rows:k1 * rows, c0:c0 + width].rearrange("(k p) n -> p k n", p=rows)
            self.slots.append((src, rows, (k1 - k0) * width))

    def rows_product(self, T, lhs, n_k, width, tiles, first_bank, user, rows=P):
        chunks = w_chunks(n_k)
        for k0, k1 in chunks:
            slot = self.tile_begins(T)
            w = self.ring[0:rows, slot, 0:(k1 - k0) * width].rearrange("p (k n) -> p k n", n=width)
            for n, t in enumerate(tiles):
                b = (first_bank + n) % BANKS
                if k0 == 0:
                    T.engine.wait_ge(*T.freed(b))
                for k in range(k0, k1):
                    ins = self.mm(T, self.ps[:, b, 0:width], lhs(k, t), w[:, k - k0, :],
                                  k == 0, k == n_k - 1)
                if k1 == n_k:
                    ins.then_inc(self.sem("psum_for_" + user(t)), 1)
                    T.hand([b], user(t))
        return (first_bank + len(tiles)) % BANKS


    def sync_stream(self, S):
        n = 0
        for entry in self.slots:
            if entry == "s5_stored":
                S.engine.wait_ge(self.sem("ends_stored"), S.due("ends_stored", 16 * (G // GB)))
                S.engine.wait_ge(self.sem("inside_stored"), S.due("inside_stored", 32 * (G // GB) * CL))
                S.engine.wait_ge(self.sem("from_state_stored"), S.due("from_state_stored", 32 * (G // GB)))
                continue
            if len(entry) == 3:
                src, rows, size = entry
                if n >= SLOTS:
                    S.engine.wait_ge(self.sem("weights_used"), n - SLOTS + 2)
                dst = self.ring[0:rows, n % SLOTS, 0:size].rearrange("p (k n) -> p k n", n=src.shape[2])
                S.engine.dma_start(dst, src).then_inc(self.sem(f"slot{n % SLOTS}_loaded"), 16)
                n += 1
                continue
            count, tiles = entry
            first = 0
            if n < SLOTS:
                for u in range(SLOTS):
                    src = tiles[u](0)
                    dst = self.ring[:, (n + u) % SLOTS, 0:SLOT].rearrange("p (k n) -> p k n", n=src.shape[2])
                    S.engine.dma_start(dst, src).then_inc(self.sem(f"slot{(n + u) % SLOTS}_loaded"), 16)
                first = 1
            with S.engine.Fori(first, count) as i:
                for u in range(SLOTS):
                    src = tiles[u](i)
                    dst = self.ring[:, (n + u) % SLOTS, 0:SLOT].rearrange("p (k n) -> p k n", n=src.shape[2])
                    S.engine.wait_ge(self.sem("weights_used"), i * SLOTS + (n + u - SLOTS + 2))
                    S.engine.dma_start(dst, src).then_inc(self.sem(f"slot{(n + u) % SLOTS}_loaded"), 16)
            n += count * SLOTS


    def vector_start(self, V):
        V.engine.sem_inc(self.sem("vector_released"), BANKS)
        V.seen["vector_released"] = BANKS

    def scalar_start(self, A):
        A.engine.sem_inc(self.sem("scalar_released"), BANKS)
        A.seen["scalar_released"] = BANKS
        a, e, n = self.a, A.engine, 0
        rows = [(a["c"], 8), (a["c_ctx"].rearrange("(a d) -> a d", a=1), 8), (a["norm1_g"], 16),
                (a["norm2_g"], 16), (a["s5_d"], 8), (a["mla_q_norm_g"], 2), (a["mla_kv_norm_g"], 1)]
        at = 0
        for src, k in rows:
            e.dma_start(self.raw[at:at + k, 0, :], src.rearrange("a (k n) -> (a k) n", n=P))\
                .then_inc(self.sem("constants_loaded"), 16)
            at += k
            n += 1
        e.dma_start(self.raw[0:96, 1, :], a["ada_b"].rearrange("l (k n) -> (l k) n", n=P))\
            .then_inc(self.sem("constants_loaded"), 16)
        for dst, name in ((self.ident, "identity"), (self.rope_mla, "rope_mla"), (self.rope_ret, "rope_ret"),
                          (self.lag, "lag"), (self.dlen, "decay_lengths")):
            e.dma_start(dst[:], a[name]).then_inc(self.sem("constants_loaded"), 16)
            n += 1
        for t in range(TT):
            src = a["x"] if t < TL else a["ctx"]
            r = (t % TL) * P
            e.dma_start(self.x[:, t, :], src[0, r:r + P, :]).then_inc(self.sem("x_loaded"), 16)
        for j, name in enumerate(("mla_qn_g", "mla_kn_g")):
            e.dma_start(self.gains[:, j, :], a[name].to_broadcast([P, QK])).then_inc(self.sem("constants_loaded"), 16)
        for j, name in enumerate(("ret_lg_f", "ret_lg_b")):
            e.dma_start(self.lgr[:, 0, j * H:(j + 1) * H], a[name].to_broadcast([P, H]))\
                .then_inc(self.sem("constants_loaded"), 16)
        self.n_constants = (n + 1 + 4) * 16

    def tensor_vectors(self, T):
        T.engine.wait_ge(self.sem("constants_loaded"), T.due("constants_loaded", self.n_constants))
        ins = T.engine.transpose(self.ps[:, 0, 0:59], self.raw[0:59, 0, :], self.ident[0:59, 0:59])
        ins = T.engine.transpose(self.ps[:, 1, 0:96], self.raw[0:96, 1, :], self.ident[0:96, 0:96])
        ins.then_inc(self.sem("psum_for_vector"), 1)
        T.hand([0, 1], "vector")

    def vector_vectors(self, V):
        V.engine.wait_ge(self.sem("psum_for_vector"), V.due("psum_for_vector"))
        V.engine.tensor_copy(self.colp[:, 0:59], self.ps[:, 0, 0:59]).then_inc(self.sem("vector_step"), 1)
        V.engine.wait_ge(self.sem("vector_step"), V.due("vector_step"))
        V.engine.tensor_copy(self.adab[:, :], self.ps[:, 1, 0:96]).then_inc(self.sem("vector_released"), 1)
        V.engine.wait_ge(self.sem("vector_released"), V.due("vector_released"))
        V.engine.tensor_copy(self.sm[:, 0:16], self.colp[:, 0:16]).then_inc(self.sem("c_ready"), 1)
        V.engine.wait_ge(self.sem("c_ready"), V.due("c_ready"))

    def scalar_vectors(self, A):
        A.engine.wait_ge(self.sem("c_ready"), A.due("c_ready"))
        A.engine.activation(self.cs[:, :, :], self.sm[:, 0:16].rearrange("p (c k) -> p k c", k=KT),
                                   ACT.Silu).then_inc(self.sem("silu_c_ready"), 1)
        A.engine.wait_ge(self.sem("silu_c_ready"), A.due("silu_c_ready"))

    def list_ada(self, l):
        def tile(u):
            return lambda i: self.a["ada_w"][l, :, ds(i * (SLOTS * 256) + u * 256, 256)]\
                .rearrange("(k p) n -> p k n", p=P)
        self.slots.append((CHUNKS * D // 256 // SLOTS, [tile(u) for u in range(SLOTS)]))

    def tensor_ada(self, T):
        for b in range(BANKS):
            T.engine.wait_ge(*T.freed(b))
        with T.bank_loop(6, SLOTS, **{f"slot{u}_loaded": 16 for u in range(SLOTS)}):
            for u in range(SLOTS):
                slot = self.tile_begins(T)
                w = self.ring[:, slot, :].rearrange("p (k n) -> p k n", n=256)
                T.engine.wait_ge(self.sem("vector_released"), T.place_freed(u + 1))
                for j in range(2):
                    for k in range(KT):
                        ins = self.mm(T, self.ps[:, u, 2 * j:2 * j + 2], w[:, k, j * P:(j + 1) * P],
                                      self.cs[:, k, :], k == 0, k == KT - 1)
                ins.then_inc(self.sem("psum_for_vector"), 1)
                T.hand([u], "vector")

    def load_rows_of_columns(self, w, width):
        for c in range(0, width, 256):
            self.slots.append((w[:, c:c + 256].rearrange("(k p) n -> p k n", p=P), P, SLOT))

    def tensor_ada_tile(self, T, n):
        slot, b = self.tile_begins(T), n % 4
        w = self.ring[:, slot, :].rearrange("p (k n) -> p k n", n=256)
        T.engine.wait_ge(*T.freed(b))
        for j in range(2):
            for k in range(KT):
                ins = self.mm(T, self.ps[:, b, 2 * j:2 * j + 2], w[:, k, j * P:(j + 1) * P],
                              self.cs[:, k, :], k == 0, k == KT - 1)
        ins.then_inc(self.sem("psum_for_vector"), 1)
        T.hand([b], "vector")

    def vector_ada_tile(self, V, l, n):
        V.engine.wait_ge(self.sem("psum_for_vector"), V.due("psum_for_vector"))
        V.engine.tensor_tensor(
            self.modT[:, l, 2 * n:2 * n + 2, :], self.ps[:, n % 4, 0:4].rearrange("p (j c) -> p j c", c=2),
            self.adab[:, l * 48 + 2 * n:l * 48 + 2 * n + 2].unsqueeze(2).to_broadcast([P, 2, 2]), ALU.add)\
            .then_inc(self.sem("vector_released"), 1)
        V.engine.wait_ge(self.sem("vector_released"), V.due("vector_released"))

    def vector_ada(self, V, l):
        with V.loop(6, psum_for_vector=SLOTS, vector_released=SLOTS) as i:
            for u in range(SLOTS):
                V.engine.wait_ge(self.sem("psum_for_vector"), V.due("psum_for_vector"))
                V.engine.tensor_tensor(
                    self.modT[:, l, ds(i * 8 + 2 * u, 2), :],
                    self.ps[:, u, 0:4].rearrange("p (j c) -> p j c", c=2),
                    self.adab[:, ds(i * 8 + (l * 48 + 2 * u), 2)].unsqueeze(2).to_broadcast([P, 2, 2]), ALU.add)\
                    .then_inc(self.sem("vector_released"), 1)
                V.engine.wait_ge(self.sem("vector_released"), V.due("vector_released"))
        self.vector_norm_scales(V, l)

    def vector_norm_scales(self, V, l):
        for w in range(2):
            g = self.colp[:, 16 + 16 * w + 8 * l:24 + 16 * w + 8 * l]
            for c in range(2):
                V.engine.scalar_tensor_tensor(
                    self.normT[:, l, w, c, :], self.modT[:, l, (3 * w + 1) * KT:(3 * w + 2) * KT, c],
                    1.0, g, ALU.add, ALU.mult).then_inc(self.sem("vector_step"), 1)
                V.engine.wait_ge(self.sem("vector_step"), V.due("vector_step"))
        V.engine.tensor_copy(self.sm[:, 0:1], self.ident[:, 0:1]).then_inc(self.sem("modulation_ready"), 1)
        V.engine.wait_ge(self.sem("modulation_ready"), V.due("modulation_ready"))

    def tensor_gate(self, T, l, chunk, conds, banks):
        for c in range(conds):
            b = banks[2 * c:2 * c + 2]
            for bank in b:
                T.engine.wait_ge(*T.freed(bank))
            for k in range(KT):
                g = self.modT[:, l, chunk * KT + k, c:c + 1].to_broadcast([P, P])
                ins = T.engine.matmul(self.ps[:, b[k // 4], (k % 4) * P:(k % 4 + 1) * P], g,
                                      self.ident[:, :], start=True, stop=True)
            ins.then_inc(self.sem("psum_for_scalar"), 1)
            T.hand(b, "scalar")

    def scalar_gate(self, A, conds, banks):
        for c in range(conds):
            A.engine.wait_ge(self.sem("psum_for_scalar"), A.due("psum_for_scalar"))
            A.engine.copy(self.rowv[:, c, 0:512], self.ps[:, banks[2 * c], :])\
                .then_inc(self.sem("scalar_step"), 1)
            A.engine.wait_ge(self.sem("scalar_step"), A.due("scalar_step"))
            A.engine.copy(self.rowv[:, c, 512:D], self.ps[:, banks[2 * c + 1], :])\
                .then_inc(self.sem("scalar_released"), 1)
            A.engine.wait_ge(self.sem("scalar_released"), A.due("scalar_released"))
        A.engine.copy(self.sm[:, 500:501], self.ident[:, 0:1]).then_inc(self.sem("row_vectors_ready"), 1)
        A.engine.wait_ge(self.sem("row_vectors_ready"), A.due("row_vectors_ready"))


    def vector_rsqrt(self, V, out, in_, scale, eps):
        V.engine.tensor_scalar(out, in_, scale, eps, ALU.mult, ALU.add).then_inc(self.sem("root_asked"), 1)
        V.engine.wait_ge(self.sem("root_asked"), V.due("root_asked"))
        V.engine.wait_ge(self.sem("root_done"), V.due("root_done"))
        V.engine.reciprocal(out, out).then_inc(self.sem("vector_step"), 1)
        V.engine.wait_ge(self.sem("vector_step"), V.due("vector_step"))

    def scalar_root(self, A, ap):
        A.engine.wait_ge(self.sem("root_asked"), A.due("root_asked"))
        A.engine.activation(ap, ap, ACT.Sqrt).then_inc(self.sem("root_done"), 1)
        A.engine.wait_ge(self.sem("root_done"), A.due("root_done"))

    def scalar_rms(self, A, tiles):
        for t in tiles:
            A.engine.activation(self.xnr[:, t, :], self.x[:, t, :], ACT.Square,
                                       accum_out=self.sm[:, 16 + t:17 + t])\
                .then_inc(self.sem("scalar_step"), 1)
            A.engine.wait_ge(self.sem("scalar_step"), A.due("scalar_step"))
        A.engine.copy(self.sm[:, 24:24 + len(tiles)], self.sm[:, 16:16 + len(tiles)])\
            .then_inc(self.sem("squares_ready"), 1)
        A.engine.wait_ge(self.sem("squares_ready"), A.due("squares_ready"))
        self.scalar_root(A, self.sm[:, 32:32 + len(tiles)])

    def vector_rms(self, V, tiles):
        V.engine.wait_ge(self.sem("squares_ready"), V.due("squares_ready"))
        n = len(tiles)
        self.vector_rsqrt(V, self.sm[:, 32:32 + n], self.sm[:, 24:24 + n], 1.0 / D, EPS)
        for t in tiles:
            V.engine.tensor_scalar(self.xnr[:, t, :], self.x[:, t, :], self.sm[:, 32 + t:33 + t],
                                          None, ALU.mult).then_inc(self.sem("rows_ready"), 1)
            V.engine.wait_ge(self.sem("rows_ready"), V.due("rows_ready"))

    def tensor_turn(self, T, tiles, src, n_k=KT):
        T.engine.wait_ge(self.sem("rows_ready"), T.due("rows_ready", len(tiles)))
        for k in range(n_k):
            T.engine.wait_ge(*T.freed(k))
            for t in tiles:
                ins = T.engine.transpose(self.ps[:, k, t * P:(t + 1) * P], src(t, k), self.ident[:, :])
            ins.then_inc(self.sem("psum_for_" + ("scalar" if k % 2 else "vector")), 1)
            T.hand([k], "scalar" if k % 2 else "vector")

    def modulated(self, lane, l, w, tiles):
        s = lane.name == "scalar"
        for k in range(1 if s else 0, KT, 2):
            lane.engine.wait_ge(self.sem("psum_for_" + lane.name), lane.due("psum_for_" + lane.name))
            for c in range(2 if len(tiles) > TL else 1):
                cols = slice(c * N_LAT, (c + 1) * N_LAT)
                out, in_ = self.hT[:, k, cols], self.ps[:, k, cols]
                scale = self.normT[:, l, w, c, k:k + 1]
                shift = self.modT[:, l, 3 * w * KT + k, c:c + 1]
                if s:
                    ins = lane.engine.activation(out, in_, ACT.Identity, bias=shift, scale=scale)
                else:
                    ins = lane.engine.tensor_scalar(out, in_, scale, shift, ALU.mult, ALU.add)
            ins.then_inc(self.sem(lane.name + "_released"), 1)
            lane.engine.wait_ge(self.sem(lane.name + "_released"), lane.due(lane.name + "_released"))
        self.side(lane, "hT_from_")

    def side(self, lane, name):
        o = 504 if lane.name == "scalar" else 506
        ins = (lane.engine.copy if lane.name == "scalar" else lane.engine.tensor_copy)(
            self.sm[:, o:o + 1], self.ident[:, 0:1])
        ins.then_inc(self.sem(name + lane.name), 1)
        lane.engine.wait_ge(self.sem(name + lane.name), lane.due(name + lane.name))

    def tensor_needs_hT(self, T):
        T.engine.wait_ge(self.sem("hT_from_vector"), T.due("hT_from_vector"))
        T.engine.wait_ge(self.sem("hT_from_scalar"), T.due("hT_from_scalar"))


    def list_mlp1(self, l):
        def tile(u):
            return lambda i: self.a["mlp_w1"][l, :, ds(i * (SLOTS * 256) + u * 256, 256)]\
                .rearrange("(k p) n -> p k n", p=P)
        self.slots.append((D_FF // 256 // SLOTS, [tile(u) for u in range(SLOTS)]))
        for s in range(2):
            self.load_rows_of(self.a["mlp_w2"][l], D_FF // P, 512, s * 512)

    def tensor_mlp1(self, T, tiles):
        n = len(tiles) * P
        for b in range(BANKS):
            T.engine.wait_ge(*T.freed(b))
        with T.bank_loop(D_FF // 256 // SLOTS, BANKS, **{f"slot{u}_loaded": 16 for u in range(SLOTS)}):
            for u in range(SLOTS):
                slot = self.tile_begins(T)
                w = self.ring[:, slot, :].rearrange("p (k n) -> p k n", n=256)
                for j in range(2):
                    b = 2 * u + j
                    T.engine.wait_ge(self.sem("vector_released"), T.place_freed(b + 1))
                    for k in range(KT):
                        ins = self.mm(T, self.ps[:, b, 0:n], w[:, k, j * P:(j + 1) * P],
                                      self.hT[:, k, 0:n], k == 0, k == KT - 1)
                    ins.then_inc(self.sem("psum_for_vector"), 1)
                    T.hand([b], "vector")
        T.engine.wait_ge(self.sem("hidden_ready"), T.due("hidden_ready"))
        b = 0
        for s in range(2):
            b = self.rows_product(T, lambda k, t: self.h1T[:, k, t * P:(t + 1) * P], D_FF // P, 512,
                                  tiles, b, lambda t: "vector")

    def vector_mlp1(self, V, tiles):
        n = len(tiles) * P
        tmp = self.xnr[:, 0, 0:n]
        with V.loop(D_FF // 256 // SLOTS, psum_for_vector=BANKS, vector_released=BANKS,
                    vector_step=BANKS) as i:
            for b in range(BANKS):
                V.engine.wait_ge(self.sem("psum_for_vector"), V.due("psum_for_vector"))
                V.engine.tensor_scalar(tmp, self.ps[:, b, 0:n], 0.0, None, ALU.max)\
                    .then_inc(self.sem("vector_released"), 1)
                V.engine.wait_ge(self.sem("vector_released"), V.due("vector_released"))
                V.engine.tensor_tensor(self.h1T[:, ds(i * BANKS + b, 1), 0:n].rearrange("p a n -> p (a n)"),
                                              tmp, tmp, ALU.mult).then_inc(self.sem("vector_step"), 1)
                V.engine.wait_ge(self.sem("vector_step"), V.due("vector_step"))
        V.engine.tensor_copy(self.sm[:, 0:1], self.ident[:, 0:1]).then_inc(self.sem("hidden_ready"), 1)
        V.engine.wait_ge(self.sem("hidden_ready"), V.due("hidden_ready"))
        self.vector_gated(V, tiles)

    def vector_gated(self, V, tiles):
        V.engine.wait_ge(self.sem("row_vectors_ready"), V.due("row_vectors_ready"))
        b = 0
        for s in range(2):
            for t in tiles:
                V.engine.wait_ge(self.sem("psum_for_vector"), V.due("psum_for_vector"))
                tmp, x = self.xnr[:, t, 0:512], self.x[:, t, s * 512:(s + 1) * 512]
                g = self.rowv[:, 0 if t < TL else 1, s * 512:(s + 1) * 512]
                V.engine.tensor_tensor(tmp, self.ps[:, b, :], g, ALU.mult)\
                    .then_inc(self.sem("vector_released"), 1)
                V.engine.wait_ge(self.sem("vector_released"), V.due("vector_released"))
                V.engine.tensor_tensor(x, x, tmp, ALU.add).then_inc(self.sem("vector_step"), 1)
                V.engine.wait_ge(self.sem("vector_step"), V.due("vector_step"))
                b = (b + 1) % BANKS
        V.engine.tensor_copy(self.sm[:, 0:1], self.ident[:, 0:1]).then_inc(self.sem("x_ready"), 1)
        V.engine.wait_ge(self.sem("x_ready"), V.due("x_ready"))


    def list_mixer1(self):
        a = self.a
        for s in range(0, IN_W, 512):
            self.load_rows_of(a["w_in"][0], KT, min(512, IN_W - s), s)
        self.load_rows_of(a["mla_w_uq"][0], 2, H * QK)
        self.load_rows_of(a["mla_w_ukv"][0], 1, H * P)
        for s in range(2):
            self.load_rows_of(a["w_out"][0], KT, 512, s * 512)

    @staticmethod
    def by_parity(t):
        return "scalar" if t % 2 else "vector"

    def tensor_z(self, T):
        self.tensor_needs_hT(T)
        b = 0
        for s in range(0, IN_W, 512):
            b = self.rows_product(T, lambda k, t: self.hT[:, k, t * P:(t + 1) * P], KT,
                                  min(512, IN_W - s), range(TT), b, self.by_parity)

    def copy(self, lane, out, in_):
        return (lane.engine.copy if lane.name == "scalar" else lane.engine.tensor_copy)(out, in_)

    def drain_z(self, lane, z, width, n_tiles):
        b = 0
        for s in range(0, width, 512):
            w = min(512, width - s)
            for t in range(n_tiles):
                if self.by_parity(t) == lane.name:
                    lane.engine.wait_ge(self.sem("psum_for_" + lane.name), lane.due("psum_for_" + lane.name))
                    self.copy(lane, z[:, t, s:s + w], self.ps[:, b, 0:w])\
                        .then_inc(self.sem(lane.name + "_released"), 1)
                    lane.engine.wait_ge(self.sem(lane.name + "_released"), lane.due(lane.name + "_released"))
                b = (b + 1) % BANKS
        self.side(lane, "z_from_")

    def scalar_gamma(self, A):
        g, e = self.lgr, A.engine
        A.engine.wait_ge(self.sem("constants_loaded"), A.due("constants_loaded", self.n_constants))
        e.activation(g[:, 1, :], g[:, 0, :], ACT.Exp, scale=float(np.log(2.0)))\
            .then_inc(self.sem("gamma_power"), 1)
        A.engine.wait_ge(self.sem("gamma_power"), A.due("gamma_power"))
        A.engine.wait_ge(self.sem("gamma_rest"), A.due("gamma_rest"))
        e.activation(g[:, 4, :], g[:, 2, :], ACT.Ln).then_inc(self.sem("gamma_log"), 1)
        A.engine.wait_ge(self.sem("gamma_log"), A.due("gamma_log"))
        A.engine.wait_ge(self.sem("gamma_lengths"), A.due("gamma_lengths"))
        e.activation(self.dec[:, :, :, :], self.dec[:, :, :, :], ACT.Exp)\
            .then_inc(self.sem("decays_ready"), 1)
        A.engine.wait_ge(self.sem("decays_ready"), A.due("decays_ready"))

    def vector_gamma(self, V):
        g, e = self.lgr, V.engine
        V.engine.wait_ge(self.sem("gamma_power"), V.due("gamma_power"))
        e.tensor_scalar(g[:, 2, :], g[:, 1, :], -1.0, 1.0, ALU.mult, ALU.add)\
            .then_inc(self.sem("gamma_rest"), 1)
        V.engine.wait_ge(self.sem("gamma_rest"), V.due("gamma_rest"))
        e.tensor_scalar(g[:, 3, :], g[:, 2, :], -1.0, None, ALU.add).then_inc(self.sem("vector_step"), 1)
        V.engine.wait_ge(self.sem("vector_step"), V.due("vector_step"))
        e.tensor_scalar(g[:, 5, :], g[:, 3, :], 0.0, None, ALU.is_equal).then_inc(self.sem("vector_step"), 1)
        V.engine.wait_ge(self.sem("vector_step"), V.due("vector_step"))
        e.tensor_tensor(g[:, 3, :], g[:, 3, :], g[:, 5, :], ALU.subtract).then_inc(self.sem("vector_step"), 1)
        V.engine.wait_ge(self.sem("vector_step"), V.due("vector_step"))
        e.reciprocal(g[:, 3, :], g[:, 3, :]).then_inc(self.sem("vector_step"), 1)
        V.engine.wait_ge(self.sem("vector_step"), V.due("vector_step"))
        V.engine.wait_ge(self.sem("gamma_log"), V.due("gamma_log"))
        e.tensor_tensor(g[:, 4, :], g[:, 4, :], g[:, 3, :], ALU.mult).then_inc(self.sem("vector_step"), 1)
        V.engine.wait_ge(self.sem("vector_step"), V.due("vector_step"))
        e.tensor_tensor(g[:, 4, :], g[:, 4, :], g[:, 5, :], ALU.add).then_inc(self.sem("vector_step"), 1)
        V.engine.wait_ge(self.sem("vector_step"), V.due("vector_step"))
        e.scalar_tensor_tensor(g[:, 5, :], g[:, 4, :], -1.0, g[:, 1, :], ALU.mult, ALU.mult)\
            .then_inc(self.sem("vector_step"), 1)
        V.engine.wait_ge(self.sem("vector_step"), V.due("vector_step"))
        lg = g[:, 5, :].rearrange("p (c h) -> p h c", c=2).unsqueeze(1).to_broadcast([P, 4, H, 2])
        n = self.dlen[:, :, :].unsqueeze(2).to_broadcast([P, 4, H, 2])
        e.tensor_tensor(self.dec[:, :, :, :], lg, n, ALU.mult).then_inc(self.sem("gamma_lengths"), 1)
        V.engine.wait_ge(self.sem("gamma_lengths"), V.due("gamma_lengths"))
        V.engine.wait_ge(self.sem("decays_ready"), V.due("decays_ready"))

    def vector_lora_norms(self, V):
        V.engine.wait_ge(self.sem("z_from_scalar"), V.due("z_from_scalar"))
        e = V.engine
        sq = self.aux[:, 0:TT * 384].rearrange("p (t n) -> p t n", t=TT)
        z = self.z[:, :, 0:384]
        e.tensor_tensor(sq, z, z, ALU.mult).then_inc(self.sem("vector_step"), 1)
        V.engine.wait_ge(self.sem("vector_step"), V.due("vector_step"))
        e.tensor_reduce(self.sm[:, 40:44], sq[:, :, 0:Q_LORA], AX.X, ALU.add)\
            .then_inc(self.sem("vector_step"), 1)
        V.engine.wait_ge(self.sem("vector_step"), V.due("vector_step"))
        e.tensor_reduce(self.sm[:, 44:48], sq[:, :, Q_LORA:384], AX.X, ALU.add)\
            .then_inc(self.sem("vector_step"), 1)
        V.engine.wait_ge(self.sem("vector_step"), V.due("vector_step"))
        e.tensor_scalar(self.sm[:, 40:44], self.sm[:, 40:44], KV_LORA / Q_LORA, None, ALU.mult)\
            .then_inc(self.sem("vector_step"), 1)
        V.engine.wait_ge(self.sem("vector_step"), V.due("vector_step"))
        self.vector_rsqrt(V, self.sm[:, 40:48], self.sm[:, 40:48], 1.0 / KV_LORA, EPS)
        zn = self.xn[:, 0:TT * 384].rearrange("p (t n) -> p t n", t=TT)
        e.tensor_tensor(zn[:, :, 0:Q_LORA], z[:, :, 0:Q_LORA],
                               self.sm[:, 40:44].unsqueeze(2).to_broadcast([P, TT, Q_LORA]), ALU.mult)\
            .then_inc(self.sem("vector_step"), 1)
        V.engine.wait_ge(self.sem("vector_step"), V.due("vector_step"))
        e.tensor_tensor(zn[:, :, Q_LORA:384], z[:, :, Q_LORA:384],
                               self.sm[:, 44:48].unsqueeze(2).to_broadcast([P, TT, KV_LORA]), ALU.mult)\
            .then_inc(self.sem("lora_rows"), 1)
        V.engine.wait_ge(self.sem("lora_rows"), V.due("lora_rows"))
        for k in range(3):
            V.engine.wait_ge(self.sem("psum_for_vector"), V.due("psum_for_vector"))
            e.tensor_scalar(self.aux[:, 1536 + k * 512:2048 + k * 512], self.ps[:, k, :],
                                      self.colp[:, 56 + k:57 + k], None, ALU.mult)\
                .then_inc(self.sem("vector_released"), 1)
            V.engine.wait_ge(self.sem("vector_released"), V.due("vector_released"))
        e.tensor_copy(self.sm[:, 0:1], self.ident[:, 0:1]).then_inc(self.sem("lora_columns"), 1)
        V.engine.wait_ge(self.sem("lora_columns"), V.due("lora_columns"))

    def tensor_lora(self, T):
        zn = self.xn[:, 0:TT * 384].rearrange("p (t n) -> p t n", t=TT)
        T.engine.wait_ge(self.sem("z_from_vector"), T.due("z_from_vector"))
        T.engine.wait_ge(self.sem("z_from_scalar"), T.due("z_from_scalar"))
        T.engine.wait_ge(self.sem("lora_rows"), T.due("lora_rows"))
        for k in range(3):
            T.engine.wait_ge(*T.freed(k))
            for t in range(TT):
                ins = T.engine.transpose(self.ps[:, k, t * P:(t + 1) * P], zn[:, t, k * P:(k + 1) * P],
                                         self.ident[:, :])
            ins.then_inc(self.sem("psum_for_vector"), 1)
            T.hand([k], "vector")
        T.engine.wait_ge(self.sem("lora_columns"), T.due("lora_columns"))
        cT = self.aux[:, 1536:3072].rearrange("p (k t) -> p k t", k=3)
        su = self.tile_begins(T)
        wq = self.ring[:, su, 0:2 * H * QK].rearrange("p (k n) -> p k n", k=2)
        for t in range(TT):
            tok = slice(t * P, (t + 1) * P)
            b = 2 * (t % 4)
            T.engine.wait_ge(*T.freed(b))
            T.engine.wait_ge(*T.freed(b + 1))
            for j, (c0, c1) in enumerate(((0, 512), (512, H * QK))):
                for k in range(2):
                    ins = self.mm(T, self.ps[:, b + j, 0:c1 - c0], cT[:, k, tok], wq[:, k, c0:c1], k == 0, k == 1)
            ins.then_inc(self.sem("psum_for_vector"), 1)
            T.hand([b, b + 1], "vector")
        su = self.tile_begins(T)
        for t in range(TT):
            tok = slice(t * P, (t + 1) * P)
            b = 2 * (t % 4)
            T.engine.wait_ge(*T.freed(b))
            T.engine.wait_ge(*T.freed(b + 1))
            for j in range(2):
                ins = self.mm(T, self.ps[:, b + j, :], cT[:, 2, tok], self.ring[:, su, j * 512:(j + 1) * 512],
                              True, True)
            ins.then_inc(self.sem("psum_for_scalar"), 1)
            T.hand([b, b + 1], "scalar")

    def scalar_kv(self, A):
        k = self.krows()
        A.engine.wait_ge(self.sem("z_from_vector"), A.due("z_from_vector"))
        for t in range(TT):
            b = 2 * (t % 4)
            A.engine.wait_ge(self.sem("psum_for_scalar"), A.due("psum_for_scalar"))
            for j in range(2):
                ins = A.engine.copy(self.kv[:, t, 4 * j:4 * j + 4, :].rearrange("p h n -> p (h n)"), self.ps[:, b + j, :])
            ins.then_inc(self.sem("scalar_released"), 1)
            A.engine.wait_ge(self.sem("scalar_released"), A.due("scalar_released"))
        for t in range(TT):
            A.engine.copy(k[:, t, :, 0:NOPE], self.kv[:, t, :, 0:NOPE]).then_inc(self.sem("scalar_step"), 1)
            A.engine.wait_ge(self.sem("scalar_step"), A.due("scalar_step"))
            kr = self.z[:, t, Q_LORA + KV_LORA:MLA_IN].unsqueeze(1).to_broadcast([P, H, ROPE])
            A.engine.copy(k[:, t, :, NOPE:QK], kr).then_inc(self.sem("k_rows"), 1)
            A.engine.wait_ge(self.sem("k_rows"), A.due("k_rows"))

    def qrows(self):
        return self.xn[:, 0:TT * H * QK].rearrange("p (t h n) -> p t h n", t=TT, h=H)

    def krows(self):
        return self.aux[:, 0:TT * H * QK].rearrange("p (t h n) -> p t h n", t=TT, h=H)

    def rotate(self, V, x, half, table, heads):
        e = V.engine
        n = TL * heads * half
        c = table[:, :, 0, :].unsqueeze(2).to_broadcast([P, TL, heads, half])
        s = table[:, :, 1, :].unsqueeze(2).to_broadcast([P, TL, heads, half])
        tmp = [self.hT[:, 2 * j:2 * j + 2, :].rearrange("p a b -> p (a b)")[:, 0:n]
               .rearrange("p (t h d) -> p t h d", t=TL, h=heads) for j in range(4)]
        x1, x2 = x[:, :, :, 0:half], x[:, :, :, half:2 * half]
        for out, in0, in1 in ((tmp[0], x1, c), (tmp[1], x2, s), (tmp[2], x1, s), (tmp[3], x2, c)):
            e.tensor_tensor(out, in0, in1, ALU.mult).then_inc(self.sem("vector_step"), 1)
            V.engine.wait_ge(self.sem("vector_step"), V.due("vector_step"))
        e.tensor_tensor(x1, tmp[0], tmp[1], ALU.subtract).then_inc(self.sem("vector_step"), 1)
        V.engine.wait_ge(self.sem("vector_step"), V.due("vector_step"))
        e.tensor_tensor(x2, tmp[2], tmp[3], ALU.add).then_inc(self.sem("vector_step"), 1)
        V.engine.wait_ge(self.sem("vector_step"), V.due("vector_step"))

    def vector_heads(self, V):
        e, q, k = V.engine, self.qrows(), self.krows()
        for t in range(TT):
            b = 2 * (t % 4)
            V.engine.wait_ge(self.sem("psum_for_vector"), V.due("psum_for_vector"))
            row = q[:, t, :, :].rearrange("p h n -> p (h n)")
            e.tensor_copy(row[:, 0:512], self.ps[:, b, :]).then_inc(self.sem("vector_step"), 1)
            V.engine.wait_ge(self.sem("vector_step"), V.due("vector_step"))
            e.tensor_copy(row[:, 512:H * QK], self.ps[:, b + 1, 0:H * QK - 512])\
                .then_inc(self.sem("vector_released"), 1)
            V.engine.wait_ge(self.sem("vector_released"), V.due("vector_released"))
        sq = self.hT[:, :, :].rearrange("p a b -> p (a b)")[:, 0:TT * H * QK].rearrange("p (m n) -> p m n", n=QK)
        for j, r in enumerate((q, k)):
            if j:
                V.engine.wait_ge(self.sem("k_rows"), V.due("k_rows", TT))
            m = r[:, :, :, :].rearrange("p t h n -> p (t h) n")
            s = self.sm[:, 64 + 32 * j:96 + 32 * j]
            e.tensor_tensor(sq, m, m, ALU.mult).then_inc(self.sem("vector_step"), 1)
            V.engine.wait_ge(self.sem("vector_step"), V.due("vector_step"))
            e.tensor_reduce(s, sq, AX.X, ALU.add).then_inc(self.sem("vector_step"), 1)
            V.engine.wait_ge(self.sem("vector_step"), V.due("vector_step"))
            self.vector_rsqrt(V, s, s, 1.0 / QK, EPS)
            e.tensor_tensor(m, m, s.unsqueeze(2).to_broadcast([P, TT * H, QK]), ALU.mult)\
                .then_inc(self.sem("vector_step"), 1)
            V.engine.wait_ge(self.sem("vector_step"), V.due("vector_step"))
            e.tensor_tensor(m, m, self.gains[:, j, :].unsqueeze(1).to_broadcast([P, TT * H, QK]), ALU.mult)\
                .then_inc(self.sem("vector_step"), 1)
            V.engine.wait_ge(self.sem("vector_step"), V.due("vector_step"))
            self.rotate(V, r[:, 0:TL, :, NOPE:QK], ROPE // 2, self.rope_mla, H)
        e.tensor_copy(self.sm[:, 0:1], self.ident[:, 0:1]).then_inc(self.sem("heads_ready"), 1)
        V.engine.wait_ge(self.sem("heads_ready"), V.due("heads_ready"))
        zr = self.z[:, 0:TL, MLA_IN:MLA_IN + 2 * RET_W].rearrange("p t (h d) -> p t h d", d=RD)
        self.rotate(V, zr, RD // 2, self.rope_ret, 2 * H)
        e.tensor_copy(self.sm[:, 0:1], self.ident[:, 0:1]).then_inc(self.sem("retention_heads_ready"), 1)
        V.engine.wait_ge(self.sem("retention_heads_ready"), V.due("retention_heads_ready"))

    KEYS = staticmethod(lambda t: range(TT) if t < TL else range(TL, TT))

    def attention_steps(self):
        return [(h, t) for h in range(H) for t in range(TT)]

    def p_of(self, n):
        return self.rowv[:, 0, (n % 2) * 512:(n % 2 + 1) * 512]

    def pT_of(self, n):
        return self.rowv[:, 1, (n % 2) * 512:(n % 2 + 1) * 512]

    def tensor_attention(self, T):
        e, steps = T.engine, self.attention_steps()
        q, k = self.qrows(), self.krows()
        T.engine.wait_ge(self.sem("heads_ready"), T.due("heads_ready"))
        for n in range(len(steps) + 2):
            if n < len(steps):
                h, t = steps[n]
                if t == 0:
                    for j, (r, user) in enumerate(((q, "vector"), (k, "scalar"))):
                        T.engine.wait_ge(*T.freed(6 + j))
                        for u in range(TT):
                            ins = e.transpose(self.ps[0:QK, 6 + j, u * P:(u + 1) * P], r[:, u, h, :], self.ident[:, :])
                        ins.then_inc(self.sem("psum_for_" + user), 1)
                        T.hand([6 + j], user)
                    T.engine.wait_ge(self.sem("qT_ready"), T.due("qT_ready"))
                    T.engine.wait_ge(self.sem("kT_ready"), T.due("kT_ready"))
                T.engine.wait_ge(*T.freed(n % 2))
                c0 = self.KEYS(t)[0] * P
                ins = e.matmul(self.ps[:, n % 2, c0:TOK], self.qkT[0:QK, h % 2, 0, t * P:(t + 1) * P],
                               self.qkT[0:QK, h % 2, 1, c0:TOK], start=True, stop=True)
                ins.then_inc(self.sem("psum_for_vector"), 1)
                T.hand([n % 2], "scalar")
            if 1 <= n <= len(steps):
                m = n - 1
                T.engine.wait_ge(self.sem("weights_scaled"), T.due("weights_scaled"))
                b = 2 + m % 2
                T.engine.wait_ge(*T.freed(b))
                for u in self.KEYS(steps[m][1]):
                    ins = e.transpose(self.ps[:, b, u * P:(u + 1) * P], self.p_of(m)[:, u * P:(u + 1) * P],
                                      self.ident[:, :])
                ins.then_inc(self.sem("psum_for_scalar"), 1)
                T.hand([b], "scalar")
            if n >= 2:
                m = n - 2
                h, t = steps[m]
                T.engine.wait_ge(self.sem("weights_turned"), T.due("weights_turned"))
                b, o = 4 + m % 2, 64 * (h % 2)
                T.engine.wait_ge(*T.freed(b))
                keys = self.KEYS(t)
                for u in keys:
                    ins = e.matmul(self.ps[o:o + V_DIM, b, 0:P], self.kv[:, u, h, NOPE:NOPE + V_DIM],
                                   self.pT_of(m)[:, u * P:(u + 1) * P], start=u == keys[0], stop=u == keys[-1])
                ins.then_inc(self.sem("psum_for_vector"), 1)
                T.hand([b], "vector")

    def vector_attention(self, V):
        e, steps = V.engine, self.attention_steps()
        for n in range(len(steps) + 2):
            if n < len(steps):
                h, t = steps[n]
                if t == 0:
                    V.engine.wait_ge(self.sem("psum_for_vector"), V.due("psum_for_vector"))
                    e.tensor_copy(self.qkT[0:QK, h % 2, 0, :], self.ps[0:QK, 6, :])\
                        .then_inc(self.sem("vector_released"), 1)
                    V.engine.wait_ge(self.sem("vector_released"), V.due("vector_released"))
                    e.tensor_copy(self.sm[:, 0:1], self.ident[:, 0:1]).then_inc(self.sem("qT_ready"), 1)
                    V.engine.wait_ge(self.sem("qT_ready"), V.due("qT_ready"))
                c0 = self.KEYS(t)[0] * P
                V.engine.wait_ge(self.sem("psum_for_vector"), V.due("psum_for_vector"))
                e.tensor_reduce(self.sm[:, 130 + n % 2:131 + n % 2], self.ps[:, n % 2, c0:TOK], AX.X, ALU.max)\
                    .then_inc(self.sem("vector_step"), 1)
                V.engine.wait_ge(self.sem("vector_step"), V.due("vector_step"))
                e.tensor_scalar(self.sm[:, 132 + n % 2:133 + n % 2], self.sm[:, 130 + n % 2:131 + n % 2],
                                       -QK ** -0.5, None, ALU.mult).then_inc(self.sem("minus_max"), 1)
                V.engine.wait_ge(self.sem("minus_max"), V.due("minus_max"))
            if 1 <= n <= len(steps):
                m = n - 1
                c0 = self.KEYS(steps[m][1])[0] * P
                V.engine.wait_ge(self.sem("weights_ready"), V.due("weights_ready"))
                e.reciprocal(self.sm[:, 136 + m % 2:137 + m % 2], self.sm[:, 134 + m % 2:135 + m % 2])\
                    .then_inc(self.sem("vector_step"), 1)
                V.engine.wait_ge(self.sem("vector_step"), V.due("vector_step"))
                e.tensor_scalar(self.p_of(m)[:, c0:TOK], self.p_of(m)[:, c0:TOK],
                                       self.sm[:, 136 + m % 2:137 + m % 2], None, ALU.mult)\
                    .then_inc(self.sem("weights_scaled"), 1)
                V.engine.wait_ge(self.sem("weights_scaled"), V.due("weights_scaled"))
            if n >= 2:
                h, t = steps[n - 2]
                o = 64 * (h % 2)
                V.engine.wait_ge(self.sem("psum_for_vector"), V.due("psum_for_vector"))
                e.tensor_copy(self.hT[o:o + V_DIM, h // 2, t * P:(t + 1) * P],
                                        self.ps[o:o + V_DIM, 4 + n % 2, 0:P])\
                    .then_inc(self.sem("vector_released"), 1)
                V.engine.wait_ge(self.sem("vector_released"), V.due("vector_released"))

    def scalar_attention(self, A):
        e, steps = A.engine, self.attention_steps()
        for n in range(len(steps) + 1):
            if n < len(steps):
                h, t = steps[n]
                if t == 0:
                    A.engine.wait_ge(self.sem("psum_for_scalar"), A.due("psum_for_scalar"))
                    e.copy(self.qkT[0:QK, h % 2, 1, :], self.ps[0:QK, 7, :])\
                        .then_inc(self.sem("scalar_released"), 1)
                    A.engine.wait_ge(self.sem("scalar_released"), A.due("scalar_released"))
                    e.copy(self.sm[:, 501:502], self.ident[:, 0:1]).then_inc(self.sem("kT_ready"), 1)
                    A.engine.wait_ge(self.sem("kT_ready"), A.due("kT_ready"))
                c0 = self.KEYS(t)[0] * P
                A.engine.wait_ge(self.sem("minus_max"), A.due("minus_max"))
                e.activation(self.p_of(n)[:, c0:TOK], self.ps[:, n % 2, c0:TOK], ACT.Exp,
                                       bias=self.sm[:, 132 + n % 2:133 + n % 2], scale=QK ** -0.5,
                                       accum_out=self.sm[:, 134 + n % 2:135 + n % 2])\
                    .then_inc(self.sem("scalar_released"), 1)
                A.engine.wait_ge(self.sem("scalar_released"), A.due("scalar_released"))
                e.copy(self.sm[:, 501:502], self.ident[:, 0:1]).then_inc(self.sem("weights_ready"), 1)
                A.engine.wait_ge(self.sem("weights_ready"), A.due("weights_ready"))
            if n >= 1:
                m = n - 1
                c0 = self.KEYS(steps[m][1])[0] * P
                A.engine.wait_ge(self.sem("psum_for_scalar"), A.due("psum_for_scalar"))
                e.copy(self.pT_of(m)[:, c0:TOK], self.ps[:, 2 + m % 2, c0:TOK])\
                    .then_inc(self.sem("scalar_released"), 1)
                A.engine.wait_ge(self.sem("scalar_released"), A.due("scalar_released"))
                e.copy(self.sm[:, 501:502], self.ident[:, 0:1]).then_inc(self.sem("weights_turned"), 1)
                A.engine.wait_ge(self.sem("weights_turned"), A.due("weights_turned"))

    def rq_columns(self, h):
        return self.aux[:, (h // 2) * TOK:(h // 2 + 1) * TOK]

    def rk_columns(self, h):
        return self.aux[:, 2048 + (h // 2 % 2) * TOK:2048 + (h // 2 % 2 + 1) * TOK]

    def decay_of(self, h):
        return self.aux[:, 3072 + (h % 2) * 384:3072 + (h % 2 + 1) * 384]

    def w_of(self, h):
        return self.rowv[:, h % 2, :].rearrange("p (g j i) -> p g j i", g=2, j=2)

    def kd(self):
        return self.xn[:, 0:2048].rearrange("p (t c n) -> p t c n", t=2, c=2)

    def state(self):
        return self.xn[:, 2048:2560].rearrange("p (m c n) -> p m c n", m=H // 2, c=2)

    def rv(self, t, h):
        o = MLA_IN + 2 * RET_W + h * RD
        return self.z[:, t, o:o + RD]

    def tensor_retention(self, T):
        e = T.engine
        T.engine.wait_ge(self.sem("decayed_keys"), T.due("decayed_keys"))
        T.engine.wait_ge(*T.freed(6))
        for h in range(H):
            o = 64 * (h % 2)
            for c in range(2):
                for t in range(2):
                    ins = e.matmul(self.ps[o:o + RD, 6, (h // 2 * 2 + c) * RD:(h // 2 * 2 + c + 1) * RD],
                                   self.kd()[:, t, c, h * RD:(h + 1) * RD], self.rv(TL + t, h),
                                   start=t == 0, stop=t == 1)
        ins.then_inc(self.sem("psum_for_vector"), 1)
        T.hand([6], "vector")
        for h in range(H):
            if h % 2 == 0:
                for j, user in enumerate(("vector", "scalar")):
                    T.engine.wait_ge(*T.freed(6 + j))
                    o = MLA_IN + j * RET_W + h * RD
                    for t in range(TT):
                        ins = e.transpose(self.ps[:, 6 + j, t * P:(t + 1) * P], self.z[:, t, o:o + P], self.ident[:, :])
                    ins.then_inc(self.sem("psum_for_" + user), 1)
                    T.hand([6 + j], user)
                T.engine.wait_ge(self.sem("rq_turned"), T.due("rq_turned"))
                T.engine.wait_ge(self.sem("rk_turned"), T.due("rk_turned"))
            o = 64 * (h % 2)
            for g in range(2):
                T.engine.wait_ge(*T.freed(4 + g))
                for j in range(2):
                    tok = (2 * g + j) * P
                    ins = e.matmul(self.ps[:, 4 + g, j * N_LAT:(j + 1) * N_LAT], self.rk_columns(h)[o:o + RD, tok:tok + P],
                                   self.rq_columns(h)[o:o + RD, g * N_LAT:(g + 1) * N_LAT], start=True, stop=True)
                ins.then_inc(self.sem("psum_for_vector"), 1)
                T.hand([4 + g], "vector")
            if h == 0:
                T.engine.wait_ge(*T.freed(0))
                T.engine.wait_ge(*T.freed(1))
                T.engine.wait_ge(*T.freed(2))
                T.engine.wait_ge(*T.freed(3))
            T.engine.wait_ge(self.sem("decayed_scores"), T.due("decayed_scores"))
            for t in range(TT):
                g = t // 2
                for j in range(2):
                    ins = e.matmul(self.ps[:, t, h * RD:(h + 1) * RD],
                                   self.w_of(h)[:, g, j, (t % 2) * P:(t % 2 + 1) * P], self.rv(2 * g + j, h),
                                   start=j == 0, stop=j == 1)
        ins.then_inc(self.sem("psum_for_vector"), 1)
        T.hand([0, 1, 2, 3], "vector")
        for t in range(TL):
            for m in range(2):
                b = 4 + 2 * t + m
                T.engine.wait_ge(*T.freed(b))
                for h in range(m, H, 2):
                    o = 64 * m
                    ins = e.matmul(self.ps[:, b, (h // 2) * P:(h // 2 + 1) * P],
                                   self.rq_columns(h)[o:o + RD, t * P:(t + 1) * P],
                                   self.state()[o:o + RD, h // 2, :, :].rearrange("p c n -> p (c n)"),
                                   start=True, stop=True)
                ins.then_inc(self.sem("psum_for_vector"), 1)
                T.hand([b], "vector")

    def scalar_retention(self, A):
        for h in range(H):
            A.engine.wait_ge(self.sem("decay_exponents"), A.due("decay_exponents"))
            A.engine.activation(self.decay_of(h), self.decay_of(h), ACT.Exp)\
                .then_inc(self.sem("decay_matrix"), 1)
            A.engine.wait_ge(self.sem("decay_matrix"), A.due("decay_matrix"))
            if h % 2 == 0:
                A.engine.wait_ge(self.sem("psum_for_scalar"), A.due("psum_for_scalar"))
                A.engine.copy(self.rk_columns(h), self.ps[:, 7, :]).then_inc(self.sem("scalar_released"), 1)
                A.engine.wait_ge(self.sem("scalar_released"), A.due("scalar_released"))
                A.engine.copy(self.sm[:, 501:502], self.ident[:, 0:1]).then_inc(self.sem("rk_turned"), 1)
                A.engine.wait_ge(self.sem("rk_turned"), A.due("rk_turned"))

    def vector_retention(self, V):
        e = V.engine
        for t in range(2):
            for c in range(2):
                k = self.z[:, TL + t, MLA_IN + RET_W:MLA_IN + 2 * RET_W].rearrange("p (h d) -> p h d", d=RD)
                e.scalar_tensor_tensor(
                    self.kd()[:, t, c, :].rearrange("p (h d) -> p h d", d=RD), k, RD ** -0.5,
                    self.dec[:, 2 + t, :, c].unsqueeze(2).to_broadcast([P, H, RD]), ALU.mult, ALU.mult)\
                    .then_inc(self.sem("vector_step"), 1)
                V.engine.wait_ge(self.sem("vector_step"), V.due("vector_step"))
        e.tensor_copy(self.sm[:, 0:1], self.ident[:, 0:1]).then_inc(self.sem("decayed_keys"), 1)
        V.engine.wait_ge(self.sem("decayed_keys"), V.due("decayed_keys"))
        V.engine.wait_ge(self.sem("psum_for_vector"), V.due("psum_for_vector"))
        e.tensor_copy(self.state().rearrange("p m c n -> p (m c n)"), self.ps[:, 6, :])\
            .then_inc(self.sem("vector_released"), 1)
        V.engine.wait_ge(self.sem("vector_released"), V.due("vector_released"))
        for h in range(H):
            d, g = self.decay_of(h), self.lgr
            e.tensor_scalar(d, self.lag[:, 1, :], g[:, 5, H + h:H + h + 1], None, ALU.mult)\
                .then_inc(self.sem("vector_step"), 1)
            V.engine.wait_ge(self.sem("vector_step"), V.due("vector_step"))
            e.scalar_tensor_tensor(d, self.lag[:, 0, :], g[:, 5, h:h + 1], d, ALU.mult, ALU.add)\
                .then_inc(self.sem("decay_exponents"), 1)
            V.engine.wait_ge(self.sem("decay_exponents"), V.due("decay_exponents"))
            if h % 2 == 0:
                V.engine.wait_ge(self.sem("psum_for_vector"), V.due("psum_for_vector"))
                e.tensor_copy(self.rq_columns(h), self.ps[:, 6, :]).then_inc(self.sem("vector_released"), 1)
                V.engine.wait_ge(self.sem("vector_released"), V.due("vector_released"))
                e.tensor_copy(self.sm[:, 0:1], self.ident[:, 0:1]).then_inc(self.sem("rq_turned"), 1)
                V.engine.wait_ge(self.sem("rq_turned"), V.due("rq_turned"))
            V.engine.wait_ge(self.sem("decay_matrix"), V.due("decay_matrix"))
            for gr in range(2):
                V.engine.wait_ge(self.sem("psum_for_vector"), V.due("psum_for_vector"))
                for j in range(2):
                    c0 = P if j == 0 else 0
                    ins = e.scalar_tensor_tensor(self.w_of(h)[:, gr, j, :], self.ps[:, 4 + gr, j * N_LAT:(j + 1) * N_LAT],
                                                 RD ** -0.5, d[:, c0:c0 + N_LAT], ALU.mult, ALU.mult)
                ins.then_inc(self.sem("vector_released"), 1)
                V.engine.wait_ge(self.sem("vector_released"), V.due("vector_released"))
            e.tensor_copy(self.sm[:, 0:1], self.ident[:, 0:1]).then_inc(self.sem("decayed_scores"), 1)
            V.engine.wait_ge(self.sem("decayed_scores"), V.due("decayed_scores"))
        V.engine.wait_ge(self.sem("psum_for_vector"), V.due("psum_for_vector"))
        for t in range(TT):
            ins = e.tensor_copy(self.ro[:, t, :, :].rearrange("p h d -> p (h d)"), self.ps[:, t, :])
        ins.then_inc(self.sem("vector_released"), 1)
        V.engine.wait_ge(self.sem("vector_released"), V.due("vector_released"))
        tmp = self.aux[:, 2048:2560]
        for t in range(TL):
            for m in range(2):
                V.engine.wait_ge(self.sem("psum_for_vector"), V.due("psum_for_vector"))
                w = self.dec[:, t, m:H:2, :].unsqueeze(3).to_broadcast([P, H // 2, 2, RD])
                four = "p (h c n) -> p h c n"
                e.tensor_tensor(tmp.rearrange(four, h=H // 2, c=2),
                                          self.ps[:, 4 + 2 * t + m, :].rearrange(four, h=H // 2, c=2), w, ALU.mult)\
                    .then_inc(self.sem("vector_released"), 1)
                V.engine.wait_ge(self.sem("vector_released"), V.due("vector_released"))
                o = self.ro[:, t, m:H:2, :]
                for c in range(2):
                    e.tensor_tensor(o, o, tmp.rearrange("p (h c n) -> p h c n", h=4, c=2)[:, :, c, :], ALU.add)\
                        .then_inc(self.sem("vector_step"), 1)
                    V.engine.wait_ge(self.sem("vector_step"), V.due("vector_step"))
        o = self.ro.rearrange("p t h d -> p (t h) d")
        s, m2 = self.sm[:, 160:192], self.sm[:, 192:224]
        sq = self.xn[:, 0:2048].rearrange("p (m d) -> p m d", d=RD)
        e.tensor_reduce(s, o, AX.X, ALU.add).then_inc(self.sem("vector_step"), 1)
        V.engine.wait_ge(self.sem("vector_step"), V.due("vector_step"))
        e.tensor_scalar(s, s, 1.0 / RD, None, ALU.mult).then_inc(self.sem("vector_step"), 1)
        V.engine.wait_ge(self.sem("vector_step"), V.due("vector_step"))
        e.tensor_tensor(o, o, s.unsqueeze(2).to_broadcast([P, TT * H, RD]), ALU.subtract)\
            .then_inc(self.sem("vector_step"), 1)
        V.engine.wait_ge(self.sem("vector_step"), V.due("vector_step"))
        e.tensor_tensor(sq, o, o, ALU.mult).then_inc(self.sem("vector_step"), 1)
        V.engine.wait_ge(self.sem("vector_step"), V.due("vector_step"))
        e.tensor_reduce(m2, sq, AX.X, ALU.add).then_inc(self.sem("vector_step"), 1)
        V.engine.wait_ge(self.sem("vector_step"), V.due("vector_step"))
        self.vector_rsqrt(V, m2, m2, 1.0 / RD, EPS)
        e.tensor_tensor(o, o, m2.unsqueeze(2).to_broadcast([P, TT * H, RD]), ALU.mult)\
            .then_inc(self.sem("vector_step"), 1)
        V.engine.wait_ge(self.sem("vector_step"), V.due("vector_step"))
        V.engine.wait_ge(self.sem("retention_gate"), V.due("retention_gate"))
        r = self.ro.rearrange("p t h d -> p t (h d)")
        gate = self.z[:, :, MLA_IN + 3 * RET_W:IN_W]
        e.tensor_tensor(r, r, gate, ALU.mult).then_inc(self.sem("retention_rows"), 1)
        V.engine.wait_ge(self.sem("retention_rows"), V.due("retention_rows"))
        for k in range(0, 4, 2):
            V.engine.wait_ge(self.sem("psum_for_vector"), V.due("psum_for_vector"))
            e.tensor_copy(self.hT[:, 4 + k, :], self.ps[:, k, :]).then_inc(self.sem("vector_released"), 1)
            V.engine.wait_ge(self.sem("vector_released"), V.due("vector_released"))
        self.side(V, "hT_from_")

    def scalar_retention_gate(self, A):
        for t in range(TT):
            g = self.z[:, t, MLA_IN + 3 * RET_W:IN_W]
            ins = A.engine.activation(g, g, ACT.Silu)
        ins.then_inc(self.sem("retention_gate"), 1)
        A.engine.wait_ge(self.sem("retention_gate"), A.due("retention_gate"))
        for k in range(1, 4, 2):
            A.engine.wait_ge(self.sem("psum_for_scalar"), A.due("psum_for_scalar"))
            A.engine.copy(self.hT[:, 4 + k, :], self.ps[:, k, :]).then_inc(self.sem("scalar_released"), 1)
            A.engine.wait_ge(self.sem("scalar_released"), A.due("scalar_released"))
        self.side(A, "hT_from_")

    def tensor_mixer1_out(self, T):
        T.engine.wait_ge(self.sem("retention_rows"), T.due("retention_rows"))
        r = self.ro.rearrange("p t h d -> p t (h d)")
        for k in range(4):
            T.engine.wait_ge(*T.freed(k))
            for t in range(TT):
                ins = T.engine.transpose(self.ps[:, k, t * P:(t + 1) * P], r[:, t, k * P:(k + 1) * P], self.ident[:, :])
            ins.then_inc(self.sem("psum_for_" + self.by_parity(k)), 1)
            T.hand([k], self.by_parity(k))
        self.tensor_gate(T, 0, 2, 2, [4, 5, 6, 7])
        self.tensor_needs_hT(T)
        b = 0
        for s in range(2):
            b = self.rows_product(T, lambda k, t: self.hT[:, k, t * P:(t + 1) * P], KT, 512, range(TT), b,
                                  lambda t: "vector")


    def s5_places(self):
        b = self.big
        self.c_raw = b[:, 0:2048].rearrange("p (k c n) -> p k c n", k=KT, c=2)
        self.pw_ends = b[:, 2048:3072].rearrange("p (c j g) -> p c j g", c=2, j=CL)
        self.pw_from_state = b[:, 3072:4096].rearrange("p (c j g) -> p c j g", c=2, j=CL)
        self.pw_lags = b[:, 4096:6016].rearrange("p (c j g) -> p c j g", c=2, j=LAGS)
        self.tmp = [b[:, 6016 + 1920 * j:7936 + 1920 * j] for j in range(2)]
        self.ends_t = b[:, 9856:11904].rearrange("p (c g n) -> p c g n", c=2, g=GB)
        self.lags = b[:, 11904:15744].rearrange("p (c g n) -> p c g n", c=2, g=GB)
        self.ends = self.aux[:, 0:2048].rearrange("p (c g n) -> p c g n", c=2, g=GB)
        self.from_state = self.aux[:, 2048:4096].rearrange("p (c g n) -> p c g n", c=2, g=GB)
        hT = self.hT[:, :, :].rearrange("p a b -> p (a b)")
        self.b_bar = hT[:, 0:2048].rearrange("p (c g n) -> p c g n", c=2, g=G)
        self.c_mat = hT[:, 2048:4096].rearrange("p (c g n) -> p c g n", c=2, g=G)
        self.kernel_lags = self.xn[0:GH, 0:GB * LAGS * GH].rearrange("p (g n) -> p g n", g=GB)
        self.a_raw = self.xn[0:G, 2048:2048 + 256].rearrange("p (c n) -> p c n", c=2)

    n_s5 = 2 * 7 * 16

    def pool_s5_loads(self, Q):
        e, a = Q.engine, self.a
        s = self.sem("s5_loaded")
        n = 0
        for d, f in enumerate("fb"):
            half = slice(d * GP, (d + 1) * GP)
            e.dma_start(self.s5p[half, 2, :], a["s5_log_dt_" + f].to_broadcast([GP, G])).then_inc(s, 16)
            for c, part in enumerate(("re", "im")):
                e.dma_start(self.a_raw[:, c, half], a[f"s5_a_{part}_{f}"][0]).then_inc(s, 16)
                src = a[f"s5_c_{part}_{f}"][0].rearrange("(k g) h p -> (g h) k p", g=GB)
                e.dma_start(self.c_raw[:, :, c, half], src).then_inc(s, 16)
                src = a[f"s5_b_{part}_{f}"][0].rearrange("g p h -> p g h")
                e.dma_start(self.b_bar[half, c, :, :], src).then_inc(s, 16)
                n += 3
            n += 1
        assert n * 16 == self.n_s5

    def tensor_s5_turns(self, T):
        T.engine.wait_ge(self.sem("s5_loaded"), T.due("s5_loaded", self.n_s5))
        T.engine.wait_ge(*T.freed(2))
        T.engine.wait_ge(*T.freed(3))
        T.engine.wait_ge(*T.freed(4))
        T.engine.wait_ge(*T.freed(5))
        T.engine.wait_ge(*T.freed(6))
        for c in range(2):
            ins = T.engine.transpose(self.ps[:, 2, c * G:(c + 1) * G], self.a_raw[:, c, :], self.ident[0:G, 0:G])
        ins.then_inc(self.sem("psum_for_vector"), 1)
        T.hand([2], "vector")
        for c in range(2):
            for k in range(KT):
                b = 3 + 2 * c + k // 4
                ins = T.engine.transpose(self.ps[:, b, (k % 4) * P:(k % 4 + 1) * P], self.c_raw[:, k, c, :],
                                         self.ident[:, :])
        ins.then_inc(self.sem("psum_for_vector"), 1)
        T.hand([3, 4, 5, 6], "vector")

    def vector_s5_parameters(self, V):
        e, s = V.engine, self.s5p
        p = lambda j: s[:, j, :]
        are, aim, dt, re, im, mag, co, si, t0, t1 = (p(j) for j in range(10))
        V.engine.wait_ge(self.sem("psum_for_vector"), V.due("psum_for_vector"))
        e.tensor_copy(s[:, 0:2, :].rearrange("p c g -> p (c g)"), self.ps[:, 2, 0:2 * G])\
            .then_inc(self.sem("vector_released"), 1)
        V.engine.wait_ge(self.sem("vector_released"), V.due("vector_released"))
        V.engine.wait_ge(self.sem("psum_for_vector"), V.due("psum_for_vector"))
        for c in range(2):
            for j in range(2):
                ins = e.tensor_copy(self.c_mat[:, c, 32 * j:32 * j + 32, :].rearrange("p g n -> p (g n)"),
                                    self.ps[:, 3 + 2 * c + j, :])
        ins.then_inc(self.sem("vector_released"), 1)
        V.engine.wait_ge(self.sem("vector_released"), V.due("vector_released"))
        e.tensor_copy(self.sm[:, 0:1], self.ident[:, 0:1]).then_inc(self.sem("s5_dt_asked"), 1)
        V.engine.wait_ge(self.sem("s5_dt_asked"), V.due("s5_dt_asked"))
        V.engine.wait_ge(self.sem("s5_dt"), V.due("s5_dt"))
        e.tensor_tensor(re, dt, are, ALU.mult).then_inc(self.sem("vector_step"), 1)
        V.engine.wait_ge(self.sem("vector_step"), V.due("vector_step"))
        e.tensor_tensor(im, dt, aim, ALU.mult).then_inc(self.sem("s5_exponent"), 1)
        V.engine.wait_ge(self.sem("s5_exponent"), V.due("s5_exponent"))
        magic = 1.5 * 2.0 ** 23
        c1 = 6.28125
        c2 = float(np.float32(np.round((TWO_PI - c1) * 2 ** 20) / 2 ** 20))
        c3 = TWO_PI - c1 - c2
        e.tensor_scalar(t0, im, 1.0 / TWO_PI, None, ALU.mult).then_inc(self.sem("vector_step"), 1)
        V.engine.wait_ge(self.sem("vector_step"), V.due("vector_step"))
        e.tensor_scalar(t0, t0, magic, None, ALU.add).then_inc(self.sem("vector_step"), 1)
        V.engine.wait_ge(self.sem("vector_step"), V.due("vector_step"))
        e.tensor_scalar(t0, t0, -magic, None, ALU.add).then_inc(self.sem("vector_step"), 1)
        V.engine.wait_ge(self.sem("vector_step"), V.due("vector_step"))
        for c in (c1, c2, c3):
            e.scalar_tensor_tensor(im, t0, -c, im, ALU.mult, ALU.add).then_inc(self.sem("vector_step"), 1)
            V.engine.wait_ge(self.sem("vector_step"), V.due("vector_step"))
        e.tensor_scalar(im, im, float(np.pi), float(-np.pi), ALU.min, ALU.max)\
            .then_inc(self.sem("vector_step"), 1)
        V.engine.wait_ge(self.sem("vector_step"), V.due("vector_step"))
        e.tensor_scalar(t1, im, 0.5, None, ALU.mult).then_inc(self.sem("s5_angle"), 1)
        V.engine.wait_ge(self.sem("s5_angle"), V.due("s5_angle"))
        V.engine.wait_ge(self.sem("s5_sines"), V.due("s5_sines"))
        e.tensor_tensor(t1, t1, t1, ALU.mult).then_inc(self.sem("vector_step"), 1)
        V.engine.wait_ge(self.sem("vector_step"), V.due("vector_step"))
        e.tensor_scalar(co, t1, -2.0, 1.0, ALU.mult, ALU.add).then_inc(self.sem("vector_step"), 1)
        V.engine.wait_ge(self.sem("vector_step"), V.due("vector_step"))
        pw = self.pw
        e.memset(pw[:, 0, 0, :], 1.0).then_inc(self.sem("vector_step"), 1)
        V.engine.wait_ge(self.sem("vector_step"), V.due("vector_step"))
        e.memset(pw[:, 1, 0, :], 0.0).then_inc(self.sem("vector_step"), 1)
        V.engine.wait_ge(self.sem("vector_step"), V.due("vector_step"))
        e.tensor_tensor(pw[:, 0, 1, :], mag, co, ALU.mult).then_inc(self.sem("vector_step"), 1)
        V.engine.wait_ge(self.sem("vector_step"), V.due("vector_step"))
        e.tensor_tensor(pw[:, 1, 1, :], mag, si, ALU.mult).then_inc(self.sem("vector_step"), 1)
        V.engine.wait_ge(self.sem("vector_step"), V.due("vector_step"))
        ar, ai = pw[:, 0, 1, :], pw[:, 1, 1, :]
        e.tensor_tensor(t0, are, are, ALU.mult).then_inc(self.sem("vector_step"), 1)
        V.engine.wait_ge(self.sem("vector_step"), V.due("vector_step"))
        e.tensor_tensor(t1, aim, aim, ALU.mult).then_inc(self.sem("vector_step"), 1)
        V.engine.wait_ge(self.sem("vector_step"), V.due("vector_step"))
        e.tensor_tensor(t0, t0, t1, ALU.add).then_inc(self.sem("vector_step"), 1)
        V.engine.wait_ge(self.sem("vector_step"), V.due("vector_step"))
        e.reciprocal(t0, t0).then_inc(self.sem("vector_step"), 1)
        V.engine.wait_ge(self.sem("vector_step"), V.due("vector_step"))
        e.tensor_scalar(re, ar, -1.0, None, ALU.add).then_inc(self.sem("vector_step"), 1)
        V.engine.wait_ge(self.sem("vector_step"), V.due("vector_step"))
        e.tensor_tensor(t1, re, are, ALU.mult).then_inc(self.sem("vector_step"), 1)
        V.engine.wait_ge(self.sem("vector_step"), V.due("vector_step"))
        e.tensor_tensor(co, ai, aim, ALU.mult).then_inc(self.sem("vector_step"), 1)
        V.engine.wait_ge(self.sem("vector_step"), V.due("vector_step"))
        e.tensor_tensor(t1, t1, co, ALU.add).then_inc(self.sem("vector_step"), 1)
        V.engine.wait_ge(self.sem("vector_step"), V.due("vector_step"))
        e.tensor_tensor(mag, t1, t0, ALU.mult).then_inc(self.sem("vector_step"), 1)
        V.engine.wait_ge(self.sem("vector_step"), V.due("vector_step"))
        e.tensor_tensor(t1, ai, are, ALU.mult).then_inc(self.sem("vector_step"), 1)
        V.engine.wait_ge(self.sem("vector_step"), V.due("vector_step"))
        e.tensor_tensor(co, re, aim, ALU.mult).then_inc(self.sem("vector_step"), 1)
        V.engine.wait_ge(self.sem("vector_step"), V.due("vector_step"))
        e.tensor_tensor(t1, t1, co, ALU.subtract).then_inc(self.sem("vector_step"), 1)
        V.engine.wait_ge(self.sem("vector_step"), V.due("vector_step"))
        e.tensor_tensor(si, t1, t0, ALU.mult).then_inc(self.sem("vector_step"), 1)
        V.engine.wait_ge(self.sem("vector_step"), V.due("vector_step"))
        w = [x.unsqueeze(2).to_broadcast([P, G, GH]) for x in (mag, si)]
        b = self.b_bar
        t = [x[:, 0:G * GH].rearrange("p (g n) -> p g n", g=G) for x in self.tmp]
        l = self.lags[:, 0, :, :].rearrange("p g n -> p (g n)")[:, 0:G * GH].rearrange("p (g n) -> p g n", g=G)
        e.tensor_tensor(t[0], b[:, 0], w[0], ALU.mult).then_inc(self.sem("vector_step"), 1)
        V.engine.wait_ge(self.sem("vector_step"), V.due("vector_step"))
        e.tensor_tensor(t[1], b[:, 1], w[1], ALU.mult).then_inc(self.sem("vector_step"), 1)
        V.engine.wait_ge(self.sem("vector_step"), V.due("vector_step"))
        e.tensor_tensor(l, t[0], t[1], ALU.subtract).then_inc(self.sem("vector_step"), 1)
        V.engine.wait_ge(self.sem("vector_step"), V.due("vector_step"))
        e.tensor_tensor(t[0], b[:, 0], w[1], ALU.mult).then_inc(self.sem("vector_step"), 1)
        V.engine.wait_ge(self.sem("vector_step"), V.due("vector_step"))
        e.tensor_tensor(t[1], b[:, 1], w[0], ALU.mult).then_inc(self.sem("vector_step"), 1)
        V.engine.wait_ge(self.sem("vector_step"), V.due("vector_step"))
        e.tensor_tensor(b[:, 1], t[0], t[1], ALU.add).then_inc(self.sem("vector_step"), 1)
        V.engine.wait_ge(self.sem("vector_step"), V.due("vector_step"))
        e.tensor_copy(b[:, 0], l).then_inc(self.sem("vector_step"), 1)
        V.engine.wait_ge(self.sem("vector_step"), V.due("vector_step"))
        for k in range(2, CL + 1):
            e.tensor_tensor(t0, pw[:, 0, k - 1, :], ar, ALU.mult).then_inc(self.sem("vector_step"), 1)
            V.engine.wait_ge(self.sem("vector_step"), V.due("vector_step"))
            e.tensor_tensor(t1, pw[:, 1, k - 1, :], ai, ALU.mult).then_inc(self.sem("vector_step"), 1)
            V.engine.wait_ge(self.sem("vector_step"), V.due("vector_step"))
            e.tensor_tensor(pw[:, 0, k, :], t0, t1, ALU.subtract).then_inc(self.sem("vector_step"), 1)
            V.engine.wait_ge(self.sem("vector_step"), V.due("vector_step"))
            e.tensor_tensor(t0, pw[:, 0, k - 1, :], ai, ALU.mult).then_inc(self.sem("vector_step"), 1)
            V.engine.wait_ge(self.sem("vector_step"), V.due("vector_step"))
            e.tensor_tensor(t1, pw[:, 1, k - 1, :], ar, ALU.mult).then_inc(self.sem("vector_step"), 1)
            V.engine.wait_ge(self.sem("vector_step"), V.due("vector_step"))
            e.tensor_tensor(pw[:, 1, k, :], t0, t1, ALU.add).then_inc(self.sem("vector_step"), 1)
            V.engine.wait_ge(self.sem("vector_step"), V.due("vector_step"))
        f, r = slice(0, GP), slice(GP, P)
        e.memset(self.pw_lags, 0.0).then_inc(self.sem("vector_step"), 1)
        V.engine.wait_ge(self.sem("vector_step"), V.due("vector_step"))
        for c in range(2):
            e.tensor_copy(self.pw_ends[f, c], pw[f, c, CL - 1::-1, :]).then_inc(self.sem("vector_step"), 1)
            V.engine.wait_ge(self.sem("vector_step"), V.due("vector_step"))
            e.tensor_copy(self.pw_ends[r, c], pw[r, c, 0:CL, :]).then_inc(self.sem("vector_step"), 1)
            V.engine.wait_ge(self.sem("vector_step"), V.due("vector_step"))
            e.tensor_copy(self.pw_from_state[f, c], pw[f, c, 1:CL + 1, :])\
                .then_inc(self.sem("vector_step"), 1)
            V.engine.wait_ge(self.sem("vector_step"), V.due("vector_step"))
            e.tensor_copy(self.pw_from_state[r, c], pw[r, c, CL:0:-1, :]).then_inc(self.sem("vector_step"), 1)
            V.engine.wait_ge(self.sem("vector_step"), V.due("vector_step"))
            e.tensor_copy(self.pw_lags[f, c, CL - 1:LAGS], pw[f, c, 0:CL, :])\
                .then_inc(self.sem("vector_step"), 1)
            V.engine.wait_ge(self.sem("vector_step"), V.due("vector_step"))
            e.tensor_copy(self.pw_lags[r, c, 0:CL], pw[r, c, CL - 1::-1, :])\
                .then_inc(self.sem("vector_step"), 1)
            V.engine.wait_ge(self.sem("vector_step"), V.due("vector_step"))

    def scalar_s5_parameters(self, A):
        e, s = A.engine, self.s5p
        A.engine.wait_ge(self.sem("s5_dt_asked"), A.due("s5_dt_asked"))
        e.activation(s[:, 2, :], s[:, 2, :], ACT.Exp).then_inc(self.sem("s5_dt"), 1)
        A.engine.wait_ge(self.sem("s5_dt"), A.due("s5_dt"))
        A.engine.wait_ge(self.sem("s5_exponent"), A.due("s5_exponent"))
        e.activation(s[:, 5, :], s[:, 3, :], ACT.Exp).then_inc(self.sem("scalar_step"), 1)
        A.engine.wait_ge(self.sem("scalar_step"), A.due("scalar_step"))
        A.engine.wait_ge(self.sem("s5_angle"), A.due("s5_angle"))
        e.activation(s[:, 7, :], s[:, 4, :], ACT.Sin).then_inc(self.sem("scalar_step"), 1)
        A.engine.wait_ge(self.sem("scalar_step"), A.due("scalar_step"))
        e.activation(s[:, 9, :], s[:, 9, :], ACT.Sin).then_inc(self.sem("s5_sines"), 1)
        A.engine.wait_ge(self.sem("s5_sines"), A.due("s5_sines"))

    def s5_product(self, V, out, powers, matrix, g0, n, sign):
        e = V.engine
        size = [P, GB, n, GH]
        pr, pi = (powers[:, c, :, g0:g0 + GB].rearrange("p j g -> p g j").unsqueeze(3).to_broadcast(size)
                  for c in range(2))
        mr, mi = (matrix[:, c, g0:g0 + GB, :].unsqueeze(2).to_broadcast(size) for c in range(2))
        t = [x[:, 0:GB * n * GH] for x in self.tmp]
        t4 = [x.rearrange("p (g j n) -> p g j n", g=GB, j=n) for x in t]
        o = [out[:, c].rearrange("p g n -> p (g n)") for c in range(2)]
        e.tensor_tensor(t4[0], pr, mr, ALU.mult).then_inc(self.sem("vector_step"), 1)
        V.engine.wait_ge(self.sem("vector_step"), V.due("vector_step"))
        e.tensor_tensor(t4[1], pi, mi, ALU.mult).then_inc(self.sem("vector_step"), 1)
        V.engine.wait_ge(self.sem("vector_step"), V.due("vector_step"))
        e.tensor_tensor(o[0], t[0], t[1], ALU.subtract).then_inc(self.sem("vector_step"), 1)
        V.engine.wait_ge(self.sem("vector_step"), V.due("vector_step"))
        e.tensor_tensor(t4[0], pr, mi, ALU.mult).then_inc(self.sem("vector_step"), 1)
        V.engine.wait_ge(self.sem("vector_step"), V.due("vector_step"))
        e.tensor_tensor(t4[1], pi, mr, ALU.mult).then_inc(self.sem("vector_step"), 1)
        V.engine.wait_ge(self.sem("vector_step"), V.due("vector_step"))
        if sign > 0:
            e.tensor_tensor(o[1], t[0], t[1], ALU.add).then_inc(self.sem("vector_step"), 1)
            V.engine.wait_ge(self.sem("vector_step"), V.due("vector_step"))
        else:
            e.scalar_tensor_tensor(o[1], t[0], -1.0, t[1], ALU.mult, ALU.subtract)\
                .then_inc(self.sem("vector_step"), 1)
            V.engine.wait_ge(self.sem("vector_step"), V.due("vector_step"))

    def vector_s5_build(self, V, gb):
        e, g0 = V.engine, gb * GB
        if gb:
            V.engine.wait_ge(self.sem("ends_turned"), V.due("ends_turned"))
        self.s5_product(V, self.ends_t, self.pw_ends, self.b_bar, g0, CL, 1)
        e.tensor_copy(self.sm[:, 0:1], self.ident[:, 0:1]).then_inc(self.sem("ends_built"), 1)
        V.engine.wait_ge(self.sem("ends_built"), V.due("ends_built"))
        if gb:
            V.engine.wait_ge(self.sem("kernel_lags_ready"), V.due("kernel_lags_ready"))
        self.s5_product(V, self.lags, self.pw_lags, self.c_mat, g0, LAGS, -1)
        e.tensor_copy(self.sm[:, 0:1], self.ident[:, 0:1]).then_inc(self.sem("lags_built"), 1)
        V.engine.wait_ge(self.sem("lags_built"), V.due("lags_built"))
        if gb:
            V.engine.wait_ge(self.sem("from_state_stored"), V.due("from_state_stored", 32))
        self.s5_product(V, self.from_state, self.pw_from_state, self.c_mat, g0, CL, -1)
        e.tensor_copy(self.sm[:, 0:1], self.ident[:, 0:1]).then_inc(self.sem("from_state_built"), 1)
        V.engine.wait_ge(self.sem("from_state_built"), V.due("from_state_built"))

    def tensor_s5_build(self, T, gb):
        g0 = gb * GB
        T.engine.wait_ge(self.sem("ends_built"), T.due("ends_built"))
        for m in range(4):
            b = 4 + m % 2
            T.engine.wait_ge(*T.freed(b))
            for j in range(4):
                c, g = divmod(4 * m + j, GB)
                ins = T.engine.transpose(self.ps[:, b, j * P:(j + 1) * P], self.ends_t[:, c, g, :], self.ident[:, :])
            ins.then_inc(self.sem("psum_for_scalar"), 1)
            T.hand([b], "scalar")
        T.engine.wait_ge(self.sem("lags_built"), T.due("lags_built"))
        for m in range(GB // 2):
            b = 4 + m % 2
            T.engine.wait_ge(*T.freed(b))
            for j in range(2):
                g = 2 * m + j
                for c in range(2):
                    ins = T.engine.matmul(self.ps[0:GH, b, j * 256:j * 256 + LAGS * GH], self.b_bar[:, c, g0 + g, :],
                                          self.lags[:, c, g, :], start=c == 0, stop=c == 1)
            ins.then_inc(self.sem("psum_for_scalar"), 1)
            T.hand([b], "scalar")

    def scalar_s5_build(self, A, gb):
        e = A.engine
        if gb:
            A.engine.wait_ge(self.sem("ends_stored"), A.due("ends_stored", 16))
        for m in range(4):
            A.engine.wait_ge(self.sem("psum_for_scalar"), A.due("psum_for_scalar"))
            c, g = divmod(4 * m, GB)
            e.copy(self.ends[:, c, g:g + 4, :].rearrange("p g n -> p (g n)"), self.ps[:, 4 + m % 2, :])\
                .then_inc(self.sem("scalar_released"), 1)
            A.engine.wait_ge(self.sem("scalar_released"), A.due("scalar_released"))
        e.copy(self.sm[:, 501:502], self.ident[:, 0:1]).then_inc(self.sem("ends_turned"), 1)
        A.engine.wait_ge(self.sem("ends_turned"), A.due("ends_turned"))
        if gb:
            A.engine.wait_ge(self.sem("inside_stored"), A.due("inside_stored", 32 * CL))
        for m in range(GB // 2):
            A.engine.wait_ge(self.sem("psum_for_scalar"), A.due("psum_for_scalar"))
            e.copy(self.kernel_lags[:, 2 * m:2 * m + 2, :],
                             self.ps[0:GH, 4 + m % 2, :].rearrange("p (g n) -> p g n", n=256)[:, :, 0:LAGS * GH])\
                .then_inc(self.sem("scalar_released"), 1)
            A.engine.wait_ge(self.sem("scalar_released"), A.due("scalar_released"))
        e.copy(self.sm[:, 501:502], self.ident[:, 0:1]).then_inc(self.sem("kernel_lags_ready"), 1)
        A.engine.wait_ge(self.sem("kernel_lags_ready"), A.due("kernel_lags_ready"))

    def pool_s5_store(self, Q, gb):
        e = Q.engine
        Q.engine.wait_ge(self.sem("ends_turned"), Q.due("ends_turned"))
        e.dma_start(self.s5_ends[gb], self.ends.rearrange("p c g n -> p (c g n)")).then_inc(self.sem("ends_stored"), 16)
        Q.engine.wait_ge(self.sem("kernel_lags_ready"), Q.due("kernel_lags_ready"))
        for j in range(CL):
            for q in range(2):
                dst = self.s5_out[gb, q, j * GH:(j + 1) * GH, 0:4 * P].rearrange("p (g n) -> p g n", n=P)
                src = self.kernel_lags[:, 4 * q:4 * q + 4, (CL - 1 - j) * GH:(CL - 1 - j) * GH + P]
                e.dma_start(dst, src).then_inc(self.sem("inside_stored"), 16)
        Q.engine.wait_ge(self.sem("from_state_built"), Q.due("from_state_built"))
        for c in range(2):
            dst = self.s5_out[gb, :, :, (1 + c) * 4 * P:(2 + c) * 4 * P].rearrange("q p n -> p q n")
            e.dma_start(dst, self.from_state[:, c].rearrange("p (q g) n -> p q (g n)", q=2))\
                .then_inc(self.sem("from_state_stored"), 16)


    def list_s5(self):
        self.slots.append("s5_stored")
        for gb in range(G // GB):
            self.slots.append((self.s5_ends[gb].unsqueeze(1), P, SLOT))
        for gb in range(G // GB):
            for q in range(2):
                self.slots.append((self.s5_out[gb, q].unsqueeze(1), P, 3 * 4 * P))
        for s in range(2):
            for half in range(2):
                self.load_rows_of(self.a["s5_w_glu"][0], KT, 512, half * D + s * 512)

    def s5_views(self):
        self.u = self.xn[:, :].rearrange("p (g c) -> p g c", g=G)
        self.xe = self.big[:, 0:8192].rearrange("p (r g c) -> p r g c", r=2, g=G)
        self.xi = self.big[:, 8192:12288].rearrange("p (r g c) -> p r g c", r=2, g=G)
        self.u_chunks = self.big[:, 12288:16384].rearrange("p (k j c) -> p k j c", k=KT, j=CL)
        self.xf = self.big[:, 0:4096].rearrange("p (r g c) -> p r g c", r=2, g=G)
        self.y_rows = self.rowv[:, :, :].rearrange("p a b -> p (a b)")
        self.yT = self.aux[:, 0:2048].rearrange("p (k i c) -> p k i c", k=KT, i=CL)
        self.ygT = self.aux[:, 2048:4096].rearrange("p (k t) -> p k t", k=KT)

    def vector_s5(self, V):
        e = V.engine
        V.engine.wait_ge(self.sem("hT_from_scalar"), V.due("hT_from_scalar", 4))
        e.tensor_copy(self.u_chunks, self.hT[:, :, :].rearrange("p k (c j) -> p k j c", j=CL))\
            .then_inc(self.sem("u_reordered"), 1)
        V.engine.wait_ge(self.sem("u_reordered"), V.due("u_reordered"))
        self.s5_drain_ends(V)
        V.engine.wait_ge(self.sem("ends_from_scalar"), V.due("ends_from_scalar"))
        s = self.sm[:, 224:480].rearrange("p (b r g) -> p b r g", b=2, r=2)
        a8 = self.pw[:, :, CL, :]
        s5 = self.s5p
        mul, cross = s5[:, 0:2, :], s5[:, 2:4, :]
        e.tensor_copy(mul[:, 0], a8[:, 0]).then_inc(self.sem("vector_step"), 1)
        V.engine.wait_ge(self.sem("vector_step"), V.due("vector_step"))
        e.tensor_copy(mul[:, 1], a8[:, 0]).then_inc(self.sem("vector_step"), 1)
        V.engine.wait_ge(self.sem("vector_step"), V.due("vector_step"))
        e.tensor_scalar(cross[:, 0], a8[:, 1], -1.0, None, ALU.mult).then_inc(self.sem("vector_step"), 1)
        V.engine.wait_ge(self.sem("vector_step"), V.due("vector_step"))
        e.tensor_copy(cross[:, 1], a8[:, 1]).then_inc(self.sem("vector_step"), 1)
        V.engine.wait_ge(self.sem("vector_step"), V.due("vector_step"))
        t0, t1 = s5[:, 4:6, :], s5[:, 6:8, :]

        def step(prev, x, out, apart=False):
            e.tensor_tensor(t0, mul, prev, ALU.mult).then_inc(self.sem("vector_step"), 1)
            V.engine.wait_ge(self.sem("vector_step"), V.due("vector_step"))
            if apart:
                e.tensor_tensor(t1[:, 0], cross[:, 0], prev[:, 1], ALU.mult)
                e.tensor_tensor(t1[:, 1], cross[:, 1], prev[:, 0], ALU.mult)\
                    .then_inc(self.sem("vector_step"), 1)
                V.engine.wait_ge(self.sem("vector_step"), V.due("vector_step"))
            else:
                e.tensor_tensor(t1, cross, prev[:, ::-1], ALU.mult).then_inc(self.sem("vector_step"), 1)
                V.engine.wait_ge(self.sem("vector_step"), V.due("vector_step"))
            e.tensor_tensor(t0, t0, t1, ALU.add).then_inc(self.sem("vector_step"), 1)
            V.engine.wait_ge(self.sem("vector_step"), V.due("vector_step"))
            e.tensor_tensor(out, t0, x, ALU.add).then_inc(self.sem("vector_step"), 1)
            V.engine.wait_ge(self.sem("vector_step"), V.due("vector_step"))

        e.tensor_copy(s[:, 0], self.xe[:, :, :, 0]).then_inc(self.sem("vector_step"), 1)
        V.engine.wait_ge(self.sem("vector_step"), V.due("vector_step"))
        with V.loop((NCH - NCH_L - 2) // 2, vector_step=8) as i:
            for u in range(2):
                x = self.xe[:, :, :, ds(2 * i + 1 + u, 1)].rearrange("p r g c -> p r (g c)")
                step(s[:, u], x, s[:, 1 - u])
        step(s[:, 0], self.xe[:, :, :, NCH - NCH_L - 1], self.xi[:, :, :, 0])
        with V.loop(NCH_L - 1, vector_step=4) as i:
            prev, out = (self.xi[:, :, :, ds(i + j, 1)].rearrange("p r g c -> p r (g c)") for j in range(2))
            x = self.xe[:, :, :, ds(i + (NCH - NCH_L), 1)].rearrange("p r g c -> p r (g c)")
            step(prev, x, out, apart=True)
        e.tensor_copy(self.xf[0:GP], self.xi[0:GP]).then_inc(self.sem("vector_step"), 1)
        V.engine.wait_ge(self.sem("vector_step"), V.due("vector_step"))
        e.tensor_copy(self.xf[GP:P], self.xi[GP:P, :, :, ::-1]).then_inc(self.sem("states_ready"), 1)
        V.engine.wait_ge(self.sem("states_ready"), V.due("states_ready"))
        self.s5_drain_y(V)
        V.engine.wait_ge(self.sem("y_turned"), V.due("y_turned", 16 * self.n_y))
        for k in range(KT):
            e.scalar_tensor_tensor(
                self.ygT[:, k].rearrange("p (c i) -> p c i", i=CL),
                self.hT[:, k, 0:N_LAT].rearrange("p (c i) -> p c i", i=CL),
                self.colp[:, 48 + k:49 + k], self.yT[:, k].rearrange("p i c -> p c i"),
                ALU.mult, ALU.add).then_inc(self.sem("y_with_skip"), 1)
            V.engine.wait_ge(self.sem("y_with_skip"), V.due("y_with_skip"))

    def s5_drain_ends(self, lane):
        for gb in range(G // GB):
            for r in range(2):
                if (r == 0) != (lane.name == "vector"):
                    continue
                lane.engine.wait_ge(self.sem("psum_for_" + lane.name), lane.due("psum_for_" + lane.name))
                b = (2 * gb + r) % BANKS
                src = self.ps[:, b, :].rearrange("p (g c) -> p g c", g=GB)
                dst = self.xe[:, r, gb * GB:(gb + 1) * GB, :]
                self.copy(lane, dst[0:GP, :, 0:NCH - NCH_L], src[0:GP, :, NCH_L:NCH])
                self.copy(lane, dst[0:GP, :, NCH - NCH_L:NCH], src[0:GP, :, 0:NCH_L])
                self.copy(lane, dst[GP:P], src[GP:P, :, ::-1]).then_inc(self.sem(lane.name + "_released"), 1)
                lane.engine.wait_ge(self.sem(lane.name + "_released"), lane.due(lane.name + "_released"))
        if lane.name == "scalar":
            self.side(lane, "ends_from_")

    def s5_drain_y(self, lane):
        for gb in range(G // GB):
            if self.by_parity(gb) == lane.name:
                lane.engine.wait_ge(self.sem("psum_for_" + lane.name), lane.due("psum_for_" + lane.name))
                self.copy(lane, self.y_rows[:, gb * 256:(gb + 1) * 256], self.ps[:, gb, 0:256])\
                    .then_inc(self.sem(lane.name + "_released"), 1)
                lane.engine.wait_ge(self.sem(lane.name + "_released"), lane.due(lane.name + "_released"))
        self.side(lane, "y_from_")

    def pool_s5(self, Q):
        e = Q.engine
        Q.engine.wait_ge(self.sem("u_reordered"), Q.due("u_reordered"))
        e.dma_start(self.scratch.rearrange("(k p) j c -> p k (j c)", p=P),
                    self.u_chunks.rearrange("p k j c -> p k (j c)")).then_inc(self.sem("u_stored"), 16)
        Q.engine.wait_ge(self.sem("u_stored"), Q.due("u_stored", 16))
        src = self.scratch.rearrange("(g h) j c -> j h g c", h=GH)
        for j in range(CL):
            e.dma_start(self.u[j * GH:(j + 1) * GH], src[j]).then_inc(self.sem("u_turned"), 16)
        Q.engine.wait_ge(self.sem("y_from_vector"), Q.due("y_from_vector"))
        Q.engine.wait_ge(self.sem("y_from_scalar"), Q.due("y_from_scalar"))
        e.dma_start(self.scratch_y, self.y_rows).then_inc(self.sem("y_stored"), 16)
        Q.engine.wait_ge(self.sem("y_stored"), Q.due("y_stored", 16))
        src = self.scratch_y.rearrange("(i h) (k g c) -> g k h i c", h=GH, k=KT, g=GB)
        for g in range(GB):
            for k in range(KT):
                e.dma_start(self.yT[g * GH:(g + 1) * GH, k], src[g, k]).then_inc(self.sem("y_turned"), 16)
    n_y = GB * KT

    def tensor_s5(self, T):
        e = T.engine
        T.engine.wait_ge(self.sem("u_turned"), T.due("u_turned", 16 * CL))
        for gb in range(G // GB):
            slot = self.tile_begins(T)
            w = self.ring[:, slot, :].rearrange("p (r g n) -> p r g n", r=2, g=GB)
            for r in range(2):
                b = (2 * gb + r) % BANKS
                T.engine.wait_ge(*T.freed(b))
                for g in range(GB):
                    ins = self.mm(T, self.ps[:, b, g * NCH:(g + 1) * NCH], w[:, r, g, :], self.u[:, gb * GB + g, :],
                                  True, True)
                ins.then_inc(self.sem("psum_for_" + ("vector" if r == 0 else "scalar")), 1)
                T.hand([b], "vector" if r == 0 else "scalar")
        T.engine.wait_ge(self.sem("states_ready"), T.due("states_ready"))
        for gb in range(G // GB):
            T.engine.wait_ge(*T.freed(gb))
            for q in range(2):
                slot = self.tile_begins(T)
                w = self.ring[:, slot, 0:3 * 4 * P].rearrange("p (r g n) -> p r g n", r=3, g=4)
                for j in range(4):
                    g = gb * GB + 4 * q + j
                    out = self.ps[:, gb, (4 * q + j) * NCH_L:(4 * q + j + 1) * NCH_L]
                    self.mm(T, out, w[:, 0, j, :], self.u[:, g, 0:NCH_L], True, False)
                    for r in range(2):
                        ins = self.mm(T, out, w[:, 1 + r, j, :], self.xf[:, r, g, :], False, r == 1)
            ins.then_inc(self.sem("psum_for_" + self.by_parity(gb)), 1)
            T.hand([gb], self.by_parity(gb))

    def tensor_glu(self, T):
        T.engine.wait_ge(self.sem("glu_input"), T.due("glu_input"))
        self.tensor_gate(T, 1, 2, 1, [6, 7])
        b = 0
        for s in range(2):
            for half in range(2):
                b = self.rows_product(T, lambda k, t: self.hT[:, k, t * P:(t + 1) * P], KT, 512, range(TL), b,
                                      lambda t, half=half: "scalar" if half else "vector")

    def scalar_glu(self, A):
        e = A.engine
        for k in range(KT):
            A.engine.wait_ge(self.sem("y_with_skip"), A.due("y_with_skip"))
            ins = e.activation(self.hT[:, k, 0:N_LAT], self.ygT[:, k], ACT.Gelu_apprx_tanh)
        ins.then_inc(self.sem("glu_input"), 1)
        A.engine.wait_ge(self.sem("glu_input"), A.due("glu_input"))
        self.scalar_gate(A, 1, [6, 7])
        for s in range(2):
            for t in range(TL):
                A.engine.wait_ge(self.sem("psum_for_scalar"), A.due("psum_for_scalar"))
                e.activation(self.xnr[:, t, s * 512:(s + 1) * 512], self.ps[:, 4 * s + 2 + t, :], ACT.Sigmoid)\
                    .then_inc(self.sem("scalar_released"), 1)
                A.engine.wait_ge(self.sem("scalar_released"), A.due("scalar_released"))
                e.copy(self.sm[:, 501:502], self.ident[:, 0:1]).then_inc(self.sem("sigmoid_ready"), 1)
                A.engine.wait_ge(self.sem("sigmoid_ready"), A.due("sigmoid_ready"))

    def vector_glu(self, V):
        e = V.engine
        V.engine.wait_ge(self.sem("row_vectors_ready"), V.due("row_vectors_ready"))
        for s in range(2):
            for t in range(TL):
                V.engine.wait_ge(self.sem("psum_for_vector"), V.due("psum_for_vector"))
                V.engine.wait_ge(self.sem("sigmoid_ready"), V.due("sigmoid_ready"))
                x, tmp = (r[:, t, s * 512:(s + 1) * 512] for r in (self.x, self.xnr))
                e.tensor_tensor(tmp, self.ps[:, 4 * s + t, :], tmp, ALU.mult)\
                    .then_inc(self.sem("vector_released"), 1)
                V.engine.wait_ge(self.sem("vector_released"), V.due("vector_released"))
                e.tensor_tensor(tmp, tmp, self.rowv[:, 0, s * 512:(s + 1) * 512], ALU.mult)\
                    .then_inc(self.sem("vector_step"), 1)
                V.engine.wait_ge(self.sem("vector_step"), V.due("vector_step"))
                e.tensor_tensor(x, x, tmp, ALU.add).then_inc(self.sem("vector_step"), 1)
                V.engine.wait_ge(self.sem("vector_step"), V.due("vector_step"))
        e.tensor_copy(self.sm[:, 0:1], self.ident[:, 0:1]).then_inc(self.sem("x_ready"), 1)
        V.engine.wait_ge(self.sem("x_ready"), V.due("x_ready"))


    def list_ffn(self, gate, up, down):
        def tile(u):
            w = (gate, up)[u % 2]
            return lambda i: w[:, ds(i * 512 + (u // 2) * 256, 256)].rearrange("(k p) n -> p k n", p=P)
        pairs = D_FF2 // 256
        self.slots.append((pairs // 2, [tile(u) for u in range(SLOTS)]))
        for w in (gate, up):
            self.slots.append((w[:, (pairs - 1) * 256:].rearrange("(k p) n -> p k n", p=P), P, SLOT))
        for s in range(2):
            self.load_rows_of(down, FT2, 512, s * 512)

    def tensor_turn_x(self, T):
        T.engine.wait_ge(self.sem("x_ready"), T.due("x_ready"))
        for k in range(KT):
            T.engine.wait_ge(*T.freed(k))
            for t in range(TL):
                ins = T.engine.transpose(self.ps[:, k, t * P:(t + 1) * P], self.x[:, t, k * P:(k + 1) * P],
                                         self.ident[:, :])
            ins.then_inc(self.sem("psum_for_" + self.by_parity(k)), 1)
            T.hand([k], self.by_parity(k))

    def drain_turned(self, lane):
        for k in range(KT):
            if self.by_parity(k) == lane.name:
                lane.engine.wait_ge(self.sem("psum_for_" + lane.name), lane.due("psum_for_" + lane.name))
                self.copy(lane, self.hT[:, k, 0:N_LAT], self.ps[:, k, 0:N_LAT])\
                    .then_inc(self.sem(lane.name + "_released"), 1)
                lane.engine.wait_ge(self.sem(lane.name + "_released"), lane.due(lane.name + "_released"))
        self.side(lane, "hT_from_")

    def ffn_tile(self, T, u, looped):
        slot = self.tile_begins(T)
        w = self.ring[:, slot, :].rearrange("p (k n) -> p k n", n=256)
        for j in range(2):
            b = 2 * u + j
            if looped:
                T.engine.wait_ge(self.sem("vector_released"), T.place_freed(2 * (b // 4) + b % 2 + 1))
            else:
                T.engine.wait_ge(*T.freed(b))
            for k in range(KT):
                ins = self.mm(T, self.ps[:, b, 0:N_LAT], w[:, k, j * P:(j + 1) * P], self.hT[:, k, 0:N_LAT],
                              k == 0, k == KT - 1)
            if u % 2 == 0:
                ins.then_inc(self.sem("psum_for_scalar"), 1)
                T.held[b] = ("vector", T.given["vector"] + 1 + j)
            else:
                ins.then_inc(self.sem("psum_for_vector"), 1)
                T.hand([b], "vector")

    def tensor_ffn(self, T):
        self.tensor_needs_hT(T)
        for b in range(BANKS):
            T.engine.wait_ge(*T.freed(b))
        with T.bank_loop(D_FF2 // 512, 4, **{f"slot{u}_loaded": 16 for u in range(SLOTS)}):
            for u in range(SLOTS):
                self.ffn_tile(T, u, True)
        for u in range(2):
            self.ffn_tile(T, u, False)
        T.engine.wait_ge(self.sem("hidden_ready"), T.due("hidden_ready"))
        b = 4
        for s in range(2):
            b = self.rows_product(T, lambda k, t: self.h1T[:, k, t * P:(t + 1) * P], FT2, 512, range(TL), b,
                                  lambda t: "vector")

    def silu_of(self, j):
        return self.xnr[:, 2, j * N_LAT:(j + 1) * N_LAT]

    def scalar_ffn(self, A):
        def pair(u):
            for j in range(2):
                A.engine.wait_ge(self.sem("psum_for_scalar"), A.due("psum_for_scalar"))
                A.engine.wait_ge(self.sem("silu_used"), A.due("silu_used"))
                A.engine.activation(self.silu_of(2 * (u % 2) + j), self.ps[:, 4 * (u % 2) + j, 0:N_LAT], ACT.Silu)\
                    .then_inc(self.sem("silu_ready"), 1)
                A.engine.wait_ge(self.sem("silu_ready"), A.due("silu_ready"))
        with A.loop(D_FF2 // 512, psum_for_scalar=4, silu_ready=4, silu_used=4):
            for u in range(2):
                pair(u)
        pair(0)

    def vector_ffn(self, V):
        e = V.engine

        def pair(u, tile):
            for j in range(2):
                V.engine.wait_ge(self.sem("psum_for_vector"), V.due("psum_for_vector"))
                V.engine.wait_ge(self.sem("silu_ready"), V.due("silu_ready"))
                e.tensor_tensor(self.h1T[:, tile(2 * u + j), 0:N_LAT].rearrange("p a n -> p (a n)"),
                                          self.silu_of(2 * (u % 2) + j), self.ps[:, 4 * (u % 2) + 2 + j, 0:N_LAT],
                                          ALU.mult).then_inc(self.sem("vector_released"), 1)
                V.engine.wait_ge(self.sem("vector_released"), V.due("vector_released"))
                e.sem_inc(self.sem("silu_used"), 1)
        with V.loop(D_FF2 // 512, psum_for_vector=4, silu_ready=4, vector_released=4) as i:
            for u in range(2):
                pair(u, lambda f: ds(i * 4 + f, 1))
        pair(0, lambda f: slice(D_FF2 // 512 * 4 + f, D_FF2 // 512 * 4 + f + 1))
        e.tensor_copy(self.sm[:, 0:1], self.ident[:, 0:1]).then_inc(self.sem("hidden_ready"), 1)
        V.engine.wait_ge(self.sem("hidden_ready"), V.due("hidden_ready"))
        self.vector_add(V, 4, 0.5)

    def vector_add(self, V, b, scale):
        for t in range(TL):
            V.engine.tensor_scalar(self.x[:, t, :], self.x[:, t, :], ALPHA, None, ALU.mult)\
                .then_inc(self.sem("vector_step"), 1)
            V.engine.wait_ge(self.sem("vector_step"), V.due("vector_step"))
        for s in range(2):
            for t in range(TL):
                V.engine.wait_ge(self.sem("psum_for_vector"), V.due("psum_for_vector"))
                x = self.x[:, t, s * 512:(s + 1) * 512]
                V.engine.scalar_tensor_tensor(x, self.ps[:, b, :], scale, x, ALU.mult, ALU.add)\
                    .then_inc(self.sem("vector_released"), 1)
                V.engine.wait_ge(self.sem("vector_released"), V.due("vector_released"))
                b = (b + 1) % BANKS

    def pool_norm_rows(self, Q, g, b):
        Q.engine.wait_ge(self.sem("row_vectors_free"), Q.due("row_vectors_free"))
        for j, v in enumerate((g, b)):
            Q.engine.dma_start(self.rowv[:, j, :], v.unsqueeze(0).to_broadcast([P, D])).then_inc(self.sem("norm_rows_loaded"), 16)

    def vector_layer_norm(self, V):
        e = V.engine
        st = self.sm[:, 240:264].rearrange("p (t c n) -> p t c n", t=TL, c=2)
        mv = self.sm[:, 264:268].rearrange("p (t n) -> p t n", t=TL)
        for t in range(TL):
            for c in range(2):
                e.bn_stats(st[:, t, c, :], self.x[:, t, c * 512:(c + 1) * 512])\
                    .then_inc(self.sem("vector_step"), 1)
                V.engine.wait_ge(self.sem("vector_step"), V.due("vector_step"))
            e.bn_aggr(mv[:, t, :], st[:, t, :, :].rearrange("p c n -> p (c n)"))\
                .then_inc(self.sem("vector_step"), 1)
            V.engine.wait_ge(self.sem("vector_step"), V.due("vector_step"))
        r = self.sm[:, 268:268 + TL]
        self.vector_rsqrt(V, r, mv[:, :, 1], 1.0, LN_EPS)
        V.engine.wait_ge(self.sem("norm_rows_loaded"), V.due("norm_rows_loaded", 32))
        for t in range(TL):
            x = self.x[:, t, :]
            e.tensor_scalar(x, x, mv[:, t, 0:1], r[:, t:t + 1], ALU.subtract, ALU.mult)\
                .then_inc(self.sem("vector_step"), 1)
            V.engine.wait_ge(self.sem("vector_step"), V.due("vector_step"))
            e.tensor_tensor(x, x, self.rowv[:, 0, :], ALU.mult).then_inc(self.sem("vector_step"), 1)
            V.engine.wait_ge(self.sem("vector_step"), V.due("vector_step"))
            e.tensor_tensor(x, x, self.rowv[:, 1, :], ALU.add).then_inc(self.sem("vector_step"), 1)
            V.engine.wait_ge(self.sem("vector_step"), V.due("vector_step"))
        e.tensor_copy(self.sm[:, 0:1], self.ident[:, 0:1]).then_inc(self.sem("x_ready"), 1)
        V.engine.wait_ge(self.sem("x_ready"), V.due("x_ready"))
        e.tensor_copy(self.sm[:, 0:1], self.ident[:, 0:1]).then_inc(self.sem("row_vectors_free"), 1)
        V.engine.wait_ge(self.sem("row_vectors_free"), V.due("row_vectors_free"))


    def mixer2_views(self):
        b = self.big
        self.z2 = b[:, 0:TL * D_IN2].rearrange("p (t n) -> p t n", t=TL)
        o = TL * D_IN2
        self.zT = b[0:HD, o:o + 4096].rearrange("p (m t) -> p m t", m=16)
        o += 4096
        self.blocks = b[0:HD, o:o + 1920].rearrange("p (c g n l) -> p c g n l", c=2, g=2, n=NC)
        o += 1920
        self.pooledT = b[0:POOL_G, o:o + 1024].rearrange("p (g t) -> p g t", g=4)
        o += 1024
        self.poolT = b[:, o:o + 512].rearrange("p (k t) -> p k t", k=2)
        o += 512
        self.oT = b[0:HD, o:o + 2048].rearrange("p (h t) -> p h t", h=H)
        o += 2048
        self.gates = b[:, o:o + TL * 24].rearrange("p (t n) -> p t n", t=TL)
        o += TL * 24
        assert o <= 16384, o
        a = self.aux
        self.windows = a[:, 0:2048].rearrange("p (w s t) -> p w s t", w=4, s=TL)
        self.causal = a[:, 2048:2176]
        self.seen = a[:, 2176:2176 + TL * 2 * NC].rearrange("p (t c n) -> p t c n", t=TL, c=2)
        self.pool_w = a[0:POOL_G, 2240:2496].rearrange("p (g n) -> p g n", g=4)
        self.pool_s = a[:, 2496:2498]
        self.bg = a[:, 2500:2524]
        self.pos = a[0:CMP_L, 2524:2716].rearrange("p (c n) -> p c n", c=2)
        self.posT = a[0:HD, 2716:2780].rearrange("p (c l) -> p c l", c=2)
        self.cw2 = a[0:HD, 2780:2972].rearrange("p (c n) -> p c n", c=2)
        self.hidT = a[0:HD, 2972:3032].rearrange("p (c n) -> p c n", c=2)
        self.kcT = a[0:HD, 3032:3062]
        self.vc = a[0:NC, 3062:3254].rearrange("p (g n) -> p g n", g=2)
        self.pT2 = self.xn[:, 2048:2048 + 2 * 640].rearrange("p (b k n) -> p b k n", b=2, k=5)
        self.p2 = self.xn[:, 0:1056].rearrange("p (b n) -> p b n", b=2)

    def list_mixer2(self, l):
        a = self.a
        for s in range(0, D_IN2, 512):
            self.load_rows_of(a["w_in_2"][l], KT, min(512, D_IN2 - s), s)
        for w in (a["cmp_k_w1_2"][l], a["cmp_v_w1_2"][l]):
            for j in range(2):
                src = w[j * 16 * HD:(j + 1) * 16 * HD].rearrange("(l d) n -> d l n", d=HD)
                self.slots.append((src, HD, 16 * HD))
        for s in range(2):
            w = a["w_out_2"][l][:, s * 512:(s + 1) * 512]
            self.slots.append((w[0:POOL_W].rearrange("(k p) n -> p k n", p=P), P, 1024))
            for j in range(2):
                src = w[POOL_W + j * 4 * HD:POOL_W + (j + 1) * 4 * HD].rearrange("(k p) n -> p k n", p=HD)
                self.slots.append((src, HD, 2048))

    def pool_mixer2_loads(self, Q, l):
        e, a = Q.engine, self.a
        s = self.sem("mixer2_loaded")
        loads = [(self.pool_w, a["pool_w_2"][l].rearrange("g c d -> c g d")),
                 (self.bg, a["b_gate_2"][l:l + 1, :].to_broadcast([P, 24])),
                 (self.pos[:, 0], a["cmp_pos_k_2"][l]), (self.pos[:, 1], a["cmp_pos_v_2"][l]),
                 (self.cw2[:, 0], a["cmp_k_w2_2"][l]), (self.cw2[:, 1], a["cmp_v_w2_2"][l])]
        if l == 0:
            loads += [(self.windows, a["pool_windows"]), (self.causal, a["causal"]), (self.seen, a["seen"])]
        for dst, src in loads:
            e.dma_start(dst, src).then_inc(s, 16)
        with self.nc.allow_non_contiguous_dma(reason="256 numbers"):
            e.dma_start(self.pool_s, a["pool_scale_2"][l].rearrange("(k p) -> p k", p=P)).then_inc(s, 16)
        return 16 * (len(loads) + 1)

    def n_mixer2(self, l):
        return 16 * (10 if l == 0 else 7)

    def z2_block(self, t, m):
        o = POOL_W + m * HD if m < 14 else POOL_W + H * HD + 4 * KVW + (m - 14) * HD
        return self.z2[:, t, o:o + HD]

    def tensor_mixer2(self, T, l):
        e = T.engine
        self.tensor_needs_hT(T)
        b = 0
        for s in range(0, D_IN2, 512):
            b = self.rows_product(T, lambda k, t: self.hT[:, k, t * P:(t + 1) * P], KT, min(512, D_IN2 - s),
                                  range(TL), b, self.by_parity)
        T.engine.wait_ge(self.sem("z_from_vector"), T.due("z_from_vector"))
        T.engine.wait_ge(self.sem("z_from_scalar"), T.due("z_from_scalar"))
        T.engine.wait_ge(self.sem("mixer2_loaded"), T.due("mixer2_loaded", self.n_mixer2(l)))
        for m in range(0, 16, 2):
            b = m // 2
            T.engine.wait_ge(*T.freed(b))
            for j in range(2):
                for t in range(TL):
                    ins = e.transpose(self.ps[0:HD, b, (2 * j + t) * P:(2 * j + t + 1) * P],
                                      self.z2_block(t, m + j), self.ident[:, :])
            ins.then_inc(self.sem("psum_for_" + self.by_parity(b)), 1)
            T.hand([b], self.by_parity(b))
        T.engine.wait_ge(*T.freed(0))
        for c in range(2):
            ins = e.transpose(self.ps[0:HD, 0, c * CMP_L:(c + 1) * CMP_L], self.pos[:, c], self.ident[0:CMP_L, 0:CMP_L])
        ins.then_inc(self.sem("psum_for_vector"), 1)
        T.hand([0], "vector")
        for g in range(4):
            b = 1 + g // 2
            if g % 2 == 0:
                T.engine.wait_ge(*T.freed(b))
            for s in range(TL):
                ins = e.matmul(self.ps[0:POOL_G, b, (g % 2) * N_LAT:(g % 2 + 1) * N_LAT],
                               self.z2[:, s, g * POOL_G:(g + 1) * POOL_G], self.windows[:, g, s, :],
                               start=s == 0, stop=s == 1)
            if g % 2:
                ins.then_inc(self.sem("psum_for_scalar"), 1)
                T.hand([b], "scalar")
        T.engine.wait_ge(self.sem("pooled_ready"), T.due("pooled_ready"))
        T.engine.wait_ge(*T.freed(3))
        for g in range(4):
            o = 64 * (g % 2)
            ins = e.matmul(self.ps[o:o + POOL_G, 3, (g // 2) * N_LAT:(g // 2 + 1) * N_LAT],
                           self.pool_w[:, g, :], self.pooledT[:, g, :], start=True, stop=True)
        ins.then_inc(self.sem("psum_for_scalar"), 1)
        T.hand([3], "scalar")
        T.engine.wait_ge(self.sem("blocks_ready"), T.due("blocks_ready"))
        T.engine.wait_ge(*T.freed(4))
        for c in range(2):
            for j in range(2):
                slot = self.tile_begins(T)
                w = self.ring[0:HD, slot, 0:16 * HD].rearrange("p (l n) -> p l n", l=16)
                for i in range(16):
                    n = 16 * j + i
                    ins = self.mm(T, self.ps[0:HD, 4, c * 30:c * 30 + 30], w[:, i, :],
                                  self.blocks[:, c, :, :, n].rearrange("p g n -> p (g n)"), n == 0, n == CMP_L - 1)
        ins.then_inc(self.sem("psum_for_scalar"), 1)
        T.hand([4], "scalar")
        T.engine.wait_ge(self.sem("hidden2_ready"), T.due("hidden2_ready"))
        T.engine.wait_ge(*T.freed(5))
        e.matmul(self.ps[0:HD, 5, 0:30], self.cw2[:, 0], self.hidT[:, 0], start=True, stop=True)
        for g in range(2):
            ins = e.matmul(self.ps[0:NC, 5, 32 + g * HD:32 + (g + 1) * HD], self.hidT[:, 1, g * NC:(g + 1) * NC],
                           self.cw2[:, 1], start=True, stop=True)
        ins.then_inc(self.sem("psum_for_vector"), 1)
        T.hand([5], "vector")
        T.engine.wait_ge(self.sem("compressed_ready"), T.due("compressed_ready"))
        self.tensor_attention2(T)
        T.engine.wait_ge(self.sem("pool_mixed"), T.due("pool_mixed"))
        T.engine.wait_ge(self.sem("heads_out"), T.due("heads_out"))
        b = 0
        for s in range(2):
            T.engine.wait_ge(*T.freed(b))
            T.engine.wait_ge(*T.freed(b + 1))
            n = 0
            for rows, nk in ((P, 2), (HD, 4), (HD, 4)):
                slot = self.tile_begins(T)
                w = self.ring[0:rows, slot, 0:nk * 512].rearrange("p (k n) -> p k n", n=512)
                for t in range(TL):
                    tok = slice(t * P, (t + 1) * P)
                    for k in range(nk):
                        lhs = self.poolT[:, k, tok] if rows == P else self.oT[:, n - 2 + k, tok]
                        ins = self.mm(T, self.ps[:, b + t, :], lhs, w[:, k, :], n + k == 0, n + k == 9)
                    if n + nk == 10:
                        ins.then_inc(self.sem("psum_for_vector"), 1)
                        T.hand([b + t], "vector")
                n += nk
            b += 2

    def steps2(self):
        return [(h, t) for h in range(H) for t in range(TL)]

    def tensor_attention2(self, T):
        e, steps = T.engine, self.steps2()
        for n in range(len(steps) + 2):
            if n < len(steps):
                h, t = steps[n]
                g, b, keys = h // HPG, n % 2, (t + 1) * P
                T.engine.wait_ge(*T.freed(b))
                T.engine.wait_ge(*T.freed(2 + b))
                q = self.zT[:, h, t * P:(t + 1) * P]
                e.matmul(self.ps[:, b, 0:keys], q, self.zT[:, 12 + g, 0:keys], start=True, stop=True)
                e.matmul(self.ps[:, b, N_LAT:N_LAT + keys], q, self.zT[:, 14 + g, 0:keys], start=True, stop=True)
                ins = e.matmul(self.ps[:, 2 + b, 0:NC], q, self.kcT[:, g * NC:(g + 1) * NC], start=True, stop=True)
                ins.then_inc(self.sem("psum_for_vector"), 1)
                T.hand([b, 2 + b], "vector")
            if 1 <= n <= len(steps):
                m = n - 1
                t = steps[m][1]
                T.engine.wait_ge(self.sem("weights_scaled"), T.due("weights_scaled"))
                b, p = 4 + m % 2, self.p2[:, m % 2]
                T.engine.wait_ge(*T.freed(b))
                T.engine.wait_ge(*T.freed(b + 2))
                for c in range(2):
                    for u in range(t + 1):
                        e.transpose(self.ps[:, b, (2 * c + u) * P:(2 * c + u + 1) * P],
                                    p[:, c * N_LAT + u * P:c * N_LAT + (u + 1) * P], self.ident[:, :])
                ins = e.transpose(self.ps[0:NC, b + 2, 0:P], p[:, 512:512 + NC], self.ident[:, :])
                ins.then_inc(self.sem("psum_for_scalar"), 1)
                T.hand([b, b + 2], "scalar")
            if n >= 2:
                m = n - 2
                h, t = steps[m]
                g, b = h // HPG, 6 + m % 2
                T.engine.wait_ge(self.sem("weights_turned"), T.due("weights_turned"))
                T.engine.wait_ge(*T.freed(b))
                vs, vw = POOL_W + H * HD + 3 * KVW + g * HD, POOL_W + H * HD + 5 * KVW + g * HD
                first = True
                for c, o in enumerate((vs, vw)):
                    for u in range(t + 1):
                        e.matmul(self.ps[0:HD, b, 0:P], self.z2[:, u, o:o + HD], self.pT2[:, m % 2, 2 * c + u, :],
                                 start=first, stop=False)
                        first = False
                ins = e.matmul(self.ps[0:HD, b, 0:P], self.vc[:, g, :], self.pT2[0:NC, m % 2, 4, :],
                               start=False, stop=True)
                ins.then_inc(self.sem("psum_for_vector"), 1)
                T.hand([b], "vector")

    def vector_attention2(self, V):
        e, steps = V.engine, self.steps2()
        for n in range(len(steps) + 2):
            if n < len(steps):
                h, t = steps[n]
                b, keys = n % 2, (t + 1) * P
                p = self.p2[:, n % 2]
                V.engine.wait_ge(self.sem("psum_for_vector"), V.due("psum_for_vector"))
                both = self.ps[:, b, :].rearrange("p (c n) -> p c n", c=2)
                pb = p[:, 0:512].rearrange("p (c n) -> p c n", c=2)
                if t:
                    e.tensor_copy(pb[:, :, 0:P], both[:, :, 0:P]).then_inc(self.sem("vector_step"), 1)
                    V.engine.wait_ge(self.sem("vector_step"), V.due("vector_step"))
                e.tensor_tensor(pb[:, :, t * P:keys], both[:, :, t * P:keys],
                                       self.causal.unsqueeze(1).to_broadcast([P, 2, P]), ALU.add)\
                    .then_inc(self.sem("vector_step"), 1)
                V.engine.wait_ge(self.sem("vector_step"), V.due("vector_step"))
                e.tensor_tensor(p[:, 512:512 + NC], self.ps[:, 2 + b, 0:NC], self.seen[:, t, 0, :], ALU.add)\
                    .then_inc(self.sem("vector_released"), 1)
                V.engine.wait_ge(self.sem("vector_released"), V.due("vector_released"))
                s = self.sm[:, 300 + 3 * b:303 + 3 * b]
                e.tensor_reduce(s[:, 0:2], pb[:, :, 0:keys], AX.X, ALU.max, negate=True)\
                    .then_inc(self.sem("vector_step"), 1)
                V.engine.wait_ge(self.sem("vector_step"), V.due("vector_step"))
                e.tensor_reduce(s[:, 2:3], p[:, 512:512 + NC], AX.X, ALU.max, negate=True)\
                    .then_inc(self.sem("minus_max"), 1)
                V.engine.wait_ge(self.sem("minus_max"), V.due("minus_max"))
            if 1 <= n <= len(steps):
                m = n - 1
                h, t = steps[m]
                b, keys = m % 2, (t + 1) * P
                p = self.p2[:, b]
                s = self.sm[:, 310 + 3 * b:313 + 3 * b]
                V.engine.wait_ge(self.sem("weights_ready"), V.due("weights_ready"))
                c = p[:, 512:512 + NC]
                e.tensor_tensor(c, c, self.seen[:, t, 1, :], ALU.mult).then_inc(self.sem("vector_step"), 1)
                V.engine.wait_ge(self.sem("vector_step"), V.due("vector_step"))
                e.tensor_reduce(s[:, 2:3], c, AX.X, ALU.add).then_inc(self.sem("vector_step"), 1)
                V.engine.wait_ge(self.sem("vector_step"), V.due("vector_step"))
                e.tensor_scalar(s, s, 1e-30, None, ALU.max).then_inc(self.sem("vector_step"), 1)
                V.engine.wait_ge(self.sem("vector_step"), V.due("vector_step"))
                e.reciprocal(s, s).then_inc(self.sem("vector_step"), 1)
                V.engine.wait_ge(self.sem("vector_step"), V.due("vector_step"))
                g = self.gates[:, t, 3 * h:3 * h + 3]
                e.tensor_tensor(s[:, 0:2], s[:, 0:2], g[:, 1:3], ALU.mult)\
                    .then_inc(self.sem("vector_step"), 1)
                V.engine.wait_ge(self.sem("vector_step"), V.due("vector_step"))
                e.tensor_tensor(s[:, 2:3], s[:, 2:3], g[:, 0:1], ALU.mult)\
                    .then_inc(self.sem("vector_step"), 1)
                V.engine.wait_ge(self.sem("vector_step"), V.due("vector_step"))
                e.tensor_scalar(p[:, 0:keys], p[:, 0:keys], s[:, 0:1], None, ALU.mult)\
                    .then_inc(self.sem("vector_step"), 1)
                V.engine.wait_ge(self.sem("vector_step"), V.due("vector_step"))
                e.tensor_scalar(p[:, N_LAT:N_LAT + keys], p[:, N_LAT:N_LAT + keys], s[:, 1:2], None, ALU.mult)\
                    .then_inc(self.sem("vector_step"), 1)
                V.engine.wait_ge(self.sem("vector_step"), V.due("vector_step"))
                e.tensor_scalar(c, c, s[:, 2:3], None, ALU.mult).then_inc(self.sem("weights_scaled"), 1)
                V.engine.wait_ge(self.sem("weights_scaled"), V.due("weights_scaled"))
            if n >= 2:
                h, t = steps[n - 2]
                V.engine.wait_ge(self.sem("psum_for_vector"), V.due("psum_for_vector"))
                e.tensor_copy(self.oT[:, h, t * P:(t + 1) * P], self.ps[0:HD, 6 + n % 2, 0:P])\
                    .then_inc(self.sem("vector_released"), 1)
                V.engine.wait_ge(self.sem("vector_released"), V.due("vector_released"))
        e.tensor_copy(self.sm[:, 0:1], self.ident[:, 0:1]).then_inc(self.sem("heads_out"), 1)
        V.engine.wait_ge(self.sem("heads_out"), V.due("heads_out"))

    def scalar_attention2(self, A):
        e, steps = A.engine, self.steps2()
        for n in range(len(steps) + 1):
            if n < len(steps):
                h, t = steps[n]
                b, keys = n % 2, (t + 1) * P
                p = self.p2[:, b]
                s, r = self.sm[:, 300 + 3 * b:303 + 3 * b], self.sm[:, 310 + 3 * b:313 + 3 * b]
                A.engine.wait_ge(self.sem("minus_max"), A.due("minus_max"))
                for c in range(2):
                    x = p[:, c * N_LAT:c * N_LAT + keys]
                    e.activation(x, x, ACT.Exp, bias=s[:, c:c + 1], accum_out=r[:, c:c + 1])\
                        .then_inc(self.sem("scalar_step"), 1)
                    A.engine.wait_ge(self.sem("scalar_step"), A.due("scalar_step"))
                x = p[:, 512:512 + NC]
                e.activation(x, x, ACT.Exp, bias=s[:, 2:3]).then_inc(self.sem("weights_ready"), 1)
                A.engine.wait_ge(self.sem("weights_ready"), A.due("weights_ready"))
            if n >= 1:
                m = n - 1
                t = steps[m][1]
                A.engine.wait_ge(self.sem("psum_for_scalar"), A.due("psum_for_scalar"))
                b = 4 + m % 2
                if t:
                    e.copy(self.pT2[:, m % 2, 0:4, :].rearrange("p k n -> p (k n)"), self.ps[:, b, :])\
                        .then_inc(self.sem("scalar_step"), 1)
                    A.engine.wait_ge(self.sem("scalar_step"), A.due("scalar_step"))
                else:
                    e.copy(self.pT2[:, m % 2, 0:3:2, :],
                                  self.ps[:, b, :].rearrange("p (k n) -> p k n", k=4)[:, 0:3:2, :])\
                        .then_inc(self.sem("scalar_step"), 1)
                    A.engine.wait_ge(self.sem("scalar_step"), A.due("scalar_step"))
                e.copy(self.pT2[0:NC, m % 2, 4, :], self.ps[0:NC, b + 2, 0:P])\
                    .then_inc(self.sem("scalar_released"), 1)
                A.engine.wait_ge(self.sem("scalar_released"), A.due("scalar_released"))
                e.copy(self.sm[:, 501:502], self.ident[:, 0:1]).then_inc(self.sem("weights_turned"), 1)
                A.engine.wait_ge(self.sem("weights_turned"), A.due("weights_turned"))

    def drain_blocks(self, lane):
        for b in range(8):
            if self.by_parity(b) != lane.name:
                continue
            lane.engine.wait_ge(self.sem("psum_for_" + lane.name), lane.due("psum_for_" + lane.name))
            out = self.zT[:, 2 * b:2 * b + 2, :].rearrange("p m t -> p (m t)")
            in_ = self.ps[0:HD, b, :]
            if b >= H // 2:
                self.copy(lane, out, in_).then_inc(self.sem(lane.name + "_released"), 1)
                lane.engine.wait_ge(self.sem(lane.name + "_released"), lane.due(lane.name + "_released"))
            elif lane.name == "scalar":
                lane.engine.mul(out, in_, HD ** -0.5).then_inc(self.sem(lane.name + "_released"), 1)
                lane.engine.wait_ge(self.sem(lane.name + "_released"), lane.due(lane.name + "_released"))
            else:
                lane.engine.tensor_scalar(out, in_, HD ** -0.5, None, ALU.mult)\
                    .then_inc(self.sem(lane.name + "_released"), 1)
                lane.engine.wait_ge(self.sem(lane.name + "_released"), lane.due(lane.name + "_released"))

    def scalar_mixer2(self, A, l):
        e = A.engine
        self.drain_z(A, self.z2, D_IN2, TL)
        self.drain_blocks(A)
        A.engine.wait_ge(self.sem("z_from_vector"), A.due("z_from_vector"))
        A.engine.wait_ge(self.sem("gates_biased"), A.due("gates_biased"))
        e.activation(self.gates, self.gates, ACT.Sigmoid).then_inc(self.sem("gates_ready"), 1)
        A.engine.wait_ge(self.sem("gates_ready"), A.due("gates_ready"))
        for b in range(2):
            A.engine.wait_ge(self.sem("psum_for_scalar"), A.due("psum_for_scalar"))
            ins = e.copy(self.pooledT[:, 2 * b:2 * b + 2, :].rearrange("p g t -> p (g t)"), self.ps[0:POOL_G, 1 + b, :])
            ins.then_inc(self.sem("scalar_released"), 1)
            A.engine.wait_ge(self.sem("scalar_released"), A.due("scalar_released"))
        e.copy(self.sm[:, 501:502], self.ident[:, 0:1]).then_inc(self.sem("pooled_ready"), 1)
        A.engine.wait_ge(self.sem("pooled_ready"), A.due("pooled_ready"))
        A.engine.wait_ge(self.sem("mixer2_loaded"), A.due("mixer2_loaded", self.n_mixer2(l)))
        A.engine.wait_ge(self.sem("psum_for_scalar"), A.due("psum_for_scalar"))
        for k in range(2):
            ins = e.activation(self.poolT[:, k, :], self.ps[:, 3, k * N_LAT:(k + 1) * N_LAT], ACT.Identity,
                               scale=self.pool_s[:, k:k + 1])
        ins.then_inc(self.sem("scalar_released"), 1)
        A.engine.wait_ge(self.sem("scalar_released"), A.due("scalar_released"))
        e.copy(self.sm[:, 501:502], self.ident[:, 0:1]).then_inc(self.sem("pool_mixed"), 1)
        A.engine.wait_ge(self.sem("pool_mixed"), A.due("pool_mixed"))
        A.engine.wait_ge(self.sem("psum_for_scalar"), A.due("psum_for_scalar"))
        e.activation(self.hidT.rearrange("p c n -> p (c n)"), self.ps[0:HD, 4, 0:60], ACT.Gelu_apprx_tanh)\
            .then_inc(self.sem("scalar_released"), 1)
        A.engine.wait_ge(self.sem("scalar_released"), A.due("scalar_released"))
        e.copy(self.sm[:, 501:502], self.ident[:, 0:1]).then_inc(self.sem("hidden2_ready"), 1)
        A.engine.wait_ge(self.sem("hidden2_ready"), A.due("hidden2_ready"))
        self.scalar_attention2(A)

    def vector_mixer2(self, V, l):
        e = V.engine
        self.drain_z(V, self.z2, D_IN2, TL)
        V.engine.wait_ge(self.sem("z_from_scalar"), V.due("z_from_scalar"))
        V.engine.wait_ge(self.sem("mixer2_loaded"), V.due("mixer2_loaded", self.n_mixer2(l)))
        e.tensor_tensor(self.gates, self.z2[:, :, D_IN2 - 24:D_IN2],
                               self.bg.unsqueeze(1).to_broadcast([P, TL, 24]), ALU.add)\
            .then_inc(self.sem("gates_biased"), 1)
        V.engine.wait_ge(self.sem("gates_biased"), V.due("gates_biased"))
        self.drain_blocks(V)
        V.engine.wait_ge(self.sem("psum_for_vector"), V.due("psum_for_vector"))
        e.tensor_copy(self.posT.rearrange("p c l -> p (c l)"), self.ps[0:HD, 0, 0:2 * CMP_L])\
            .then_inc(self.sem("vector_released"), 1)
        V.engine.wait_ge(self.sem("vector_released"), V.due("vector_released"))
        V.engine.wait_ge(self.sem("gates_ready"), V.due("gates_ready"))
        for c in range(2):
            for g in range(2):
                for j in range(2):
                    x = self.zT[:, 8 + 2 * c + g, j * CMP_S:j * CMP_S + NC * CMP_S].rearrange("p (n l) -> p n l", n=NC)
                    pos = self.posT[:, c, j * CMP_S:(j + 1) * CMP_S].unsqueeze(1).to_broadcast([HD, NC, CMP_S])
                    e.tensor_tensor(self.blocks[:, c, g, :, j * CMP_S:(j + 1) * CMP_S], x, pos, ALU.add)\
                        .then_inc(self.sem("vector_step"), 1)
                    V.engine.wait_ge(self.sem("vector_step"), V.due("vector_step"))
        e.tensor_copy(self.sm[:, 0:1], self.ident[:, 0:1]).then_inc(self.sem("blocks_ready"), 1)
        V.engine.wait_ge(self.sem("blocks_ready"), V.due("blocks_ready"))
        V.engine.wait_ge(self.sem("psum_for_vector"), V.due("psum_for_vector"))
        e.tensor_copy(self.kcT, self.ps[0:HD, 5, 0:30]).then_inc(self.sem("vector_step"), 1)
        V.engine.wait_ge(self.sem("vector_step"), V.due("vector_step"))
        e.tensor_copy(self.vc, self.ps[0:NC, 5, 32:32 + 2 * HD].rearrange("p (g n) -> p g n", g=2))\
            .then_inc(self.sem("vector_released"), 1)
        V.engine.wait_ge(self.sem("vector_released"), V.due("vector_released"))
        e.tensor_copy(self.sm[:, 0:1], self.ident[:, 0:1]).then_inc(self.sem("compressed_ready"), 1)
        V.engine.wait_ge(self.sem("compressed_ready"), V.due("compressed_ready"))
        self.vector_attention2(V)
        e.tensor_copy(self.sm[:, 0:1], self.ident[:, 0:1]).then_inc(self.sem("mixer2_done"), 1)
        V.engine.wait_ge(self.sem("mixer2_done"), V.due("mixer2_done"))
        self.vector_add(V, 0, 1.0)


    def tensor_block2(self, T):
        T.engine.wait_ge(self.sem("x_ready"), T.due("x_ready", 3))
        for l in range(DEPTH):
            self.tensor_turn_x(T)
            self.tensor_ffn(T)
            self.tensor_turn_x(T)
            self.tensor_mixer2(T, l)
            self.tensor_turn_x(T)
            self.tensor_ffn(T)

    def vector_block2(self, V):
        V.engine.sem_inc(self.sem("silu_used"), 4)
        V.engine.tensor_copy(self.sm[:, 0:1], self.ident[:, 0:1]).then_inc(self.sem("row_vectors_free"), 1)
        V.engine.wait_ge(self.sem("row_vectors_free"), V.due("row_vectors_free"))
        V.engine.tensor_copy(self.sm[:, 0:1], self.ident[:, 0:1]).then_inc(self.sem("mixer2_done"), 1)
        V.engine.wait_ge(self.sem("mixer2_done"), V.due("mixer2_done"))
        for l in range(DEPTH):
            self.drain_turned(V)
            self.vector_ffn(V)
            self.vector_layer_norm(V)
            self.drain_turned(V)
            self.vector_mixer2(V, l)
            self.vector_layer_norm(V)
            self.drain_turned(V)
            self.vector_ffn(V)
            self.vector_layer_norm(V)
        V.engine.tensor_copy(self.sm[:, 0:1], self.ident[:, 0:1]).then_inc(self.sem("result_ready"), 1)
        V.engine.wait_ge(self.sem("result_ready"), V.due("result_ready"))

    def scalar_block2(self, A):
        r = self.sm[:, 268:268 + TL]
        for l in range(DEPTH):
            self.drain_turned(A)
            self.scalar_ffn(A)
            self.scalar_root(A, r)
            self.drain_turned(A)
            self.scalar_mixer2(A, l)
            self.scalar_root(A, r)
            self.drain_turned(A)
            self.scalar_ffn(A)
            self.scalar_root(A, r)

    def pool_block2(self, Q):
        a = self.a
        for l in range(DEPTH):
            self.pool_norm_rows(Q, a["ln1_g_2"][l], a["ln1_b_2"][l])
            Q.engine.wait_ge(self.sem("mixer2_done"), Q.due("mixer2_done"))
            self.pool_mixer2_loads(Q, l)
            self.pool_norm_rows(Q, a["ln2_g_2"][l], a["ln2_b_2"][l])
            self.pool_norm_rows(Q, a["ln3_g_2"][l], a["ln3_b_2"][l])


def constants():
    def on_partitions(x, tiles):
        return np.ascontiguousarray(x.reshape(tiles, P, *x.shape[1:]).swapaxes(0, 1))

    tok = np.arange(N_LAT, dtype=np.float32)
    nf = ROPE // 4
    f = (np.float32(10000.0) ** (-np.arange(nf, dtype=np.float32) / np.float32(nf))).astype(np.float32)
    ang = np.concatenate([(tok // 64)[:, None] * f, (tok % 64)[:, None] * f], axis=-1).astype(np.float32)
    nr = RD // 2
    th = (np.float32(10000.0) ** (-np.arange(nr, dtype=np.float32) / np.float32(nr))).astype(np.float32)
    ret = (tok[:, None] * th).astype(np.float32)
    diff = np.arange(3 * P)[None, :] - P - np.arange(P)[:, None]
    i = np.arange(N_LAT)
    lengths = np.stack([np.stack([i + 1, N_LAT - i], -1), np.stack([N_CTX - 1 - i, i], -1)])
    out = {
        "identity": np.eye(P),
        "rope_mla": on_partitions(np.stack([np.cos(ang), np.sin(ang)], 1), TL),
        "rope_ret": on_partitions(np.stack([np.cos(ret), np.sin(ret)], 1), TL),
        "lag": np.stack([np.maximum(diff, 0), np.maximum(-diff, 0)], 1),
        "decay_lengths": lengths.reshape(4, P, 2).swapaxes(0, 1),
    }
    t, s = i[None, :], i[:, None]
    pools = [np.where((s <= t) & (s > t - w), 1.0 / np.minimum(t + 1, w), 0.0) - (s == t) for w in WINDOWS]
    out["pool_windows"] = np.stack([on_partitions(p, TL) for p in pools], 1)
    causal = np.where(np.arange(P)[None, :] <= np.arange(P)[:, None], 0.0, NEG)
    seen = (np.arange(NC) * CMP_S + CMP_L - 1)[None, :] <= i[:, None]
    out["causal"] = causal
    out["seen"] = on_partitions(np.stack([np.where(seen, 0.0, NEG), seen], 1), TL)
    return {k: np.ascontiguousarray(v, dtype=np.float32) for k, v in out.items()}


def program(nc, a, out):
    with ExitStack() as ctx:
        K = Kernel(nc, ctx, a)
        K.list_ada(0)
        K.load_rows_of_columns(a["ada_w"][1], CHUNKS * D)
        K.list_mixer1()
        K.list_mlp1(0)
        K.list_s5()
        K.list_mlp1(1)
        for l in range(DEPTH):
            K.list_ffn(a["ffn1_w_gate_2"][l], a["ffn1_w_up_2"][l], a["ffn1_w_down_2"][l])
            K.list_mixer2(l)
            K.list_ffn(a["ffn2_w_gate_2"][l], a["ffn2_w_up_2"][l], a["ffn2_w_down_2"][l])
        block = ctx.enter_context(nc.Block())
        every, latents = range(TT), range(TL)
        normed = lambda t, k: K.xnr[:, t, k * P:(k + 1) * P]

        @block.scalar
        def _(engine):
            A = Lane("scalar", engine, K.sem)
            K.scalar_start(A)
            K.scalar_vectors(A)
            K.scalar_gamma(A)
            K.scalar_s5_parameters(A)
            for gb in range(G // GB):
                K.scalar_s5_build(A, gb)
            engine.wait_ge(K.sem("inside_stored"), A.due("inside_stored", 32 * CL))
            engine.wait_ge(K.sem("modulation_ready"), A.due("modulation_ready", 2))
            engine.wait_ge(K.sem("x_loaded"), A.due("x_loaded", 16 * TT))
            K.scalar_rms(A, every)
            K.modulated(A, 0, 0, every)
            K.drain_z(A, K.z, IN_W, TT)
            K.scalar_root(A, K.sm[:, 40:48])
            K.scalar_kv(A)
            K.scalar_root(A, K.sm[:, 64:96])
            K.scalar_root(A, K.sm[:, 96:128])
            K.scalar_attention(A)
            K.scalar_retention(A)
            K.scalar_root(A, K.sm[:, 192:224])
            K.scalar_retention_gate(A)
            K.scalar_gate(A, 2, [4, 5, 6, 7])
            engine.wait_ge(K.sem("x_ready"), A.due("x_ready"))
            K.scalar_rms(A, every)
            K.modulated(A, 0, 1, every)
            K.scalar_gate(A, 2, [0, 1, 2, 3])
            engine.wait_ge(K.sem("x_ready"), A.due("x_ready"))
            K.scalar_rms(A, every)
            K.modulated(A, 1, 0, every)
            K.s5_drain_ends(A)
            K.s5_drain_y(A)
            engine.wait_ge(K.sem("y_stored"), A.due("y_stored", 16))
            K.scalar_glu(A)
            engine.wait_ge(K.sem("x_ready"), A.due("x_ready"))
            K.scalar_rms(A, latents)
            K.modulated(A, 1, 1, latents)
            K.scalar_gate(A, 1, [0, 1])
            engine.wait_ge(K.sem("x_ready"), A.due("x_ready"))
            K.scalar_block2(A)

        @block.tensor
        def _(engine):
            T = TensorLane("tensor", engine, K.sem)
            K.tensor_vectors(T)
            K.tensor_s5_turns(T)
            engine.wait_ge(K.sem("silu_c_ready"), T.due("silu_c_ready"))
            K.tensor_ada(T)
            for gb in range(G // GB):
                for n in range(3):
                    K.tensor_ada_tile(T, 3 * gb + n)
                K.tensor_s5_build(T, gb)
            K.tensor_turn(T, every, normed)
            K.tensor_z(T)
            K.tensor_lora(T)
            K.tensor_attention(T)
            K.tensor_retention(T)
            K.tensor_mixer1_out(T)
            K.tensor_turn(T, every, normed)
            K.tensor_gate(T, 0, 5, 2, [0, 1, 2, 3])
            K.tensor_needs_hT(T)
            K.tensor_mlp1(T, every)
            K.tensor_turn(T, every, normed)
            K.tensor_needs_hT(T)
            K.tensor_s5(T)
            K.tensor_glu(T)
            K.tensor_turn(T, latents, normed)
            K.tensor_gate(T, 1, 5, 1, [0, 1])
            K.tensor_needs_hT(T)
            K.tensor_mlp1(T, latents)
            K.tensor_block2(T)

        @block.vector
        def _(engine):
            V = Lane("vector", engine, K.sem)
            K.vector_start(V)
            K.vector_vectors(V)
            K.vector_gamma(V)
            K.vector_s5_parameters(V)
            K.vector_ada(V, 0)
            for gb in range(G // GB):
                K.vector_s5_build(V, gb)
                for n in range(3):
                    K.vector_ada_tile(V, 1, 3 * gb + n)
            K.vector_norm_scales(V, 1)
            engine.wait_ge(K.sem("from_state_stored"), V.due("from_state_stored", 32))
            engine.wait_ge(K.sem("ends_stored"), V.due("ends_stored", 16 * (G // GB)))
            engine.wait_ge(K.sem("x_loaded"), V.due("x_loaded", 16 * TT))
            K.vector_rms(V, every)
            K.modulated(V, 0, 0, every)
            K.drain_z(V, K.z, IN_W, TT)
            K.vector_lora_norms(V)
            K.vector_heads(V)
            K.vector_attention(V)
            K.vector_retention(V)
            K.vector_gated(V, every)
            K.vector_rms(V, every)
            K.modulated(V, 0, 1, every)
            K.vector_mlp1(V, every)
            K.vector_rms(V, every)
            K.modulated(V, 1, 0, every)
            K.vector_s5(V)
            K.vector_glu(V)
            K.vector_rms(V, latents)
            K.modulated(V, 1, 1, latents)
            K.vector_mlp1(V, latents)
            K.vector_block2(V)

        @block.gpsimd
        def _(engine):
            Q = Lane("pool", engine, K.sem)
            K.pool_s5_loads(Q)
            for gb in range(G // GB):
                K.pool_s5_store(Q, gb)
            K.pool_s5(Q)
            K.pool_block2(Q)

        @block.sync
        def _(engine):
            S = Lane("sync", engine, K.sem)
            K.sync_stream(S)
            engine.wait_ge(K.sem("result_ready"), S.due("result_ready"))
            for t in range(TL):
                S.engine.dma_start(out[0, t * P:(t + 1) * P, :], K.x[:, t, :]).then_inc(K.sem("out_written"), 16)
            engine.wait_ge(K.sem("out_written"), S.due("out_written", 16 * TL))


def kernel(**inputs):
    import concourse.bacc as bacc
    from concourse.bass_utils import run_bass_kernel_spmd

    nc = bacc.Bacc("TRN2", target_bir_lowering=False, num_devices=1)
    arrays = {k: np.ascontiguousarray(v) for k, v in inputs.items()}
    arrays.update(constants())
    a = {k: nc.dram_tensor("in_" + k, v.shape, F32, kind="ExternalInput").ap() for k, v in arrays.items()}
    out = nc.dram_tensor("out_0", (1, N_LAT, D), F32, kind="ExternalOutput").ap()
    program(nc, a, out)
    r = run_bass_kernel_spmd(nc, [{"in_" + k: v for k, v in arrays.items()}], core_ids=[0])
    return r.results[0]["out_0"]
```
